# Optimizing a Trainium2 kernel written in Bass

```python
import jax, jax.numpy as jnp
from jax import lax
import numpy as np
import math

D_MODEL = 1024
BATCH = 1
SEQ = 256
DEPTH = 2

N_META = 16
GRID_W = 64
GLA_HEADS = 4
GLA_DK = 64
GLA_DV = 128
GLA_KEY = GLA_HEADS * GLA_DK
GLA_VAL = GLA_HEADS * GLA_DV
GLA_RANK = 16
GLA_TAU = 16.0
CHUNK = 64
ATT_HEADS = 8
ATT_KV_HEADS = 2
HEAD_DIM = 64
ATT_Q = ATT_HEADS * HEAD_DIM
ATT_KV = ATT_KV_HEADS * HEAD_DIM
Q_BLOCK = 128
ROPE_THETA = 10000.0
D_FF = 2816
EPS = 1e-6

IN_SIZES = (GLA_KEY, GLA_KEY, GLA_VAL, GLA_VAL, GLA_RANK, GLA_RANK,
            ATT_Q, ATT_KV, ATT_KV, D_MODEL, D_MODEL)
D_IN = sum(IN_SIZES)
SPLIT_POINTS = tuple(int(s) for s in np.cumsum(IN_SIZES)[:-1])


def rmsnorm(x, g):
    xf = x.astype(jnp.float32)
    y = xf * lax.rsqrt(jnp.mean(xf * xf, axis=-1, keepdims=True) + EPS)
    return (y * g.astype(jnp.float32)).astype(x.dtype)

def swiglu(x, w_gate, w_up, w_down):
    return (jax.nn.silu(x @ w_gate) * (x @ w_up)) @ w_down

def gla_causal_chunked(q, k, v, log_a):
    f32 = jnp.float32
    B, H, T, dk = q.shape
    dv = v.shape[-1]
    n = T // CHUNK
    qc = q.astype(f32).reshape(B, H, n, CHUNK, dk)
    kc = k.astype(f32).reshape(B, H, n, CHUNK, dk)
    vc = v.astype(f32).reshape(B, H, n, CHUNK, dv)
    bcum = jnp.cumsum(log_a.astype(f32).reshape(B, H, n, CHUNK, dk), axis=3)
    btot = bcum[:, :, :, -1:, :]
    q_dec = qc * jnp.exp(bcum)
    k_inv = kc * jnp.exp(-bcum)
    k_end = kc * jnp.exp(btot - bcum)
    mask = jnp.tril(jnp.ones((CHUNK, CHUNK), dtype=bool))
    att = jnp.where(mask, jnp.einsum('bhnid,bhnjd->bhnij', q_dec, k_inv), 0.0)
    o_intra = jnp.einsum('bhnij,bhnjv->bhniv', att, vc)
    kv_chunk = jnp.einsum('bhnjd,bhnjv->bhndv', k_end, vc)
    decay = jnp.exp(btot[:, :, :, 0, :])

    def step(S, inp):
        d, kv = inp
        return d[..., None] * S + kv, S

    S0 = jnp.zeros((B, H, dk, dv), f32)
    _, S_prev = lax.scan(step, S0, (jnp.moveaxis(decay, 2, 0), jnp.moveaxis(kv_chunk, 2, 0)))
    S_prev = jnp.moveaxis(S_prev, 0, 2)
    o_inter = jnp.einsum('bhnid,bhndv->bhniv', q_dec, S_prev)
    return (o_intra + o_inter).reshape(B, H, T, dv)

def gla_branch(q, k, v, r, lr_f, lr_b, w2, b2, gn_gain):
    B, L, _ = q.shape
    pad = CHUNK - N_META

    def heads(t, d):
        return t.reshape(B, L, GLA_HEADS, d).transpose(0, 2, 1, 3)

    def log_gate(lr, w, b):
        return jax.nn.log_sigmoid((lr @ w + b).astype(jnp.float32)) / GLA_TAU

    def padseq(t):
        return jnp.pad(t, ((0, 0), (0, 0), (pad, 0), (0, 0)))

    def flip(t):
        return jnp.flip(t, axis=2)

    qh = padseq(heads(q * GLA_DK ** -0.5, GLA_DK))
    kh = padseq(heads(k, GLA_DK))
    vh = padseq(heads(v, GLA_DV))
    gf = padseq(heads(log_gate(lr_f, w2[0], b2[0]), GLA_DK))
    gb = padseq(heads(log_gate(lr_b, w2[1], b2[1]), GLA_DK))
    o_f = gla_causal_chunked(qh, kh, vh, gf)
    o_b = flip(gla_causal_chunked(flip(qh), flip(kh), flip(vh), flip(gb)))
    o = (o_f + o_b)[:, :, pad:, :].transpose(0, 2, 1, 3)
    o = o * lax.rsqrt(jnp.mean(o * o, axis=-1, keepdims=True) + EPS)
    o = o.reshape(B, L, GLA_VAL) * gn_gain.astype(jnp.float32)
    return o.astype(r.dtype) * jax.nn.silu(r)

def axial_rope_tables(n_tok):
    f32 = jnp.float32
    rows = n_tok // GRID_W
    row = jnp.repeat(jnp.arange(rows), GRID_W).astype(f32)
    col = jnp.tile(jnp.arange(GRID_W), rows).astype(f32)
    axis_dim = HEAD_DIM // 2
    inv = ROPE_THETA ** (-jnp.arange(0, axis_dim, 2, dtype=f32) / axis_dim)
    ang = jnp.concatenate([row[:, None] * inv, col[:, None] * inv], axis=-1)
    ang = jnp.concatenate([jnp.zeros((N_META, axis_dim), f32), ang], axis=0)
    return jnp.cos(ang), jnp.sin(ang)

def apply_axial_rope(x, cos, sin):
    L = x.shape[-2]
    q4 = HEAD_DIM // 4
    xs = x.astype(jnp.float32).reshape(*x.shape[:-1], 2, 2, q4)
    x1, x2 = xs[..., 0, :], xs[..., 1, :]
    c = cos.reshape(L, 2, q4)
    s = sin.reshape(L, 2, q4)
    return jnp.stack([x1 * c - x2 * s, x2 * c + x1 * s], axis=-2).reshape(x.shape)

def attention_branch(q, k, v, gq, gk, cos, sin):
    B, L, _ = q.shape
    G = ATT_HEADS // ATT_KV_HEADS
    qh = q.reshape(B, L, ATT_KV_HEADS, G, HEAD_DIM).transpose(0, 2, 3, 1, 4)
    kh = k.reshape(B, L, ATT_KV_HEADS, HEAD_DIM).transpose(0, 2, 1, 3)
    vh = v.reshape(B, L, ATT_KV_HEADS, HEAD_DIM).transpose(0, 2, 1, 3)
    qh = apply_axial_rope(rmsnorm(qh, gq), cos, sin) * HEAD_DIM ** -0.5
    kh = apply_axial_rope(rmsnorm(kh, gk), cos, sin)
    pad = Q_BLOCK - N_META
    qp = jnp.pad(qh, ((0, 0), (0, 0), (0, 0), (pad, 0), (0, 0)))
    nblk = qp.shape[3] // Q_BLOCK
    qb = jnp.moveaxis(qp.reshape(B, ATT_KV_HEADS, G, nblk, Q_BLOCK, HEAD_DIM), 3, 0)

    def block(qblk):
        s = jnp.einsum('bkgqd,bksd->bkgqs', qblk, kh)
        p = jax.nn.softmax(s, axis=-1)
        return jnp.einsum('bkgqs,bksd->bkgqd', p.astype(vh.dtype), vh)

    o = lax.map(block, qb)
    o = jnp.moveaxis(o, 0, 3).reshape(B, ATT_KV_HEADS, G, nblk * Q_BLOCK, HEAD_DIM)[:, :, :, pad:]
    return o.transpose(0, 3, 1, 2, 4).reshape(B, L, ATT_Q).astype(q.dtype)

def mixer(z, w_in, gla_w2, gla_b2, gla_gn, q_norm, k_norm, w_pa, w_pb, b_merge, w_out, cos, sin):
    h = z @ w_in
    (q_a, k_a, v_a, r_a, lr_f, lr_b, q_b, k_b, v_b, g_a, g_b) = jnp.split(h, SPLIT_POINTS, axis=-1)
    a = gla_branch(q_a, k_a, v_a, r_a, lr_f, lr_b, gla_w2, gla_b2, gla_gn)
    b = attention_branch(q_b, k_b, v_b, q_norm, k_norm, cos, sin)
    y = (jax.nn.sigmoid(g_a + b_merge[0]) * (a @ w_pa)
         + jax.nn.sigmoid(g_b + b_merge[1]) * (b @ w_pb))
    return y @ w_out

def first_inputs(seed: int = 0) -> dict:
    key = jax.random.key(seed)
    ks = jax.random.split(key, 18)

    def nrm(k, shape, scale):
        return jax.random.normal(k, shape, jnp.float32) * scale

    return {
        "x": nrm(ks[0], (BATCH, SEQ, D_MODEL), 1.0),
        "meta_tokens": nrm(ks[1], (N_META, D_MODEL), 1.0),
        "norm_gains": 1.0 + nrm(ks[2], (DEPTH, 3, D_MODEL), 0.02),
        "ffn_w_gate": nrm(ks[3], (DEPTH, 2, D_MODEL, D_FF), D_MODEL ** -0.5),
        "ffn_w_up": nrm(ks[4], (DEPTH, 2, D_MODEL, D_FF), D_MODEL ** -0.5),
        "ffn_w_down": nrm(ks[5], (DEPTH, 2, D_FF, D_MODEL), D_FF ** -0.5),
        "w_in": nrm(ks[6], (DEPTH, D_MODEL, D_IN), D_MODEL ** -0.5),
        "gla_w2": nrm(ks[7], (DEPTH, 2, GLA_RANK, GLA_KEY), GLA_RANK ** -0.5),
        "gla_b2": nrm(ks[8], (DEPTH, 2, GLA_KEY), 0.1),
        "gla_gn": 1.0 + nrm(ks[9], (DEPTH, GLA_VAL), 0.02),
        "q_norm": 1.0 + nrm(ks[10], (DEPTH, HEAD_DIM), 0.02),
        "k_norm": 1.0 + nrm(ks[11], (DEPTH, HEAD_DIM), 0.02),
        "w_pa": nrm(ks[12], (DEPTH, GLA_VAL, D_MODEL), GLA_VAL ** -0.5),
        "w_pb": nrm(ks[13], (DEPTH, ATT_Q, D_MODEL), ATT_Q ** -0.5),
        "b_merge": nrm(ks[14], (DEPTH, 2, D_MODEL), 0.02),
        "w_out": nrm(ks[15], (DEPTH, D_MODEL, D_MODEL), D_MODEL ** -0.5),
        "final_norm": 1.0 + nrm(ks[16], (D_MODEL,), 0.02),
    }

def first_block(x, meta_tokens, norm_gains, ffn_w_gate, ffn_w_up, ffn_w_down, w_in, gla_w2, gla_b2,
              gla_gn, q_norm, k_norm, w_pa, w_pb, b_merge, w_out, final_norm):
    B, N, D = x.shape
    meta = jnp.broadcast_to(meta_tokens[None].astype(x.dtype), (B, N_META, D))
    h = jnp.concatenate([meta, x], axis=1)
    cos, sin = axial_rope_tables(N)
    for l in range(DEPTH):
        h = h + 0.5 * swiglu(rmsnorm(h, norm_gains[l, 0]),
                             ffn_w_gate[l, 0], ffn_w_up[l, 0], ffn_w_down[l, 0])
        h = h + mixer(rmsnorm(h, norm_gains[l, 1]), w_in[l], gla_w2[l], gla_b2[l], gla_gn[l],
                      q_norm[l], k_norm[l], w_pa[l], w_pb[l], b_merge[l], w_out[l], cos, sin)
        h = h + 0.5 * swiglu(rmsnorm(h, norm_gains[l, 2]),
                             ffn_w_gate[l, 1], ffn_w_up[l, 1], ffn_w_down[l, 1])
    return rmsnorm(h, final_norm)[:, N_META:]


POOL_WINDOWS = (2, 4, 8, 16)
N_POOL_GROUPS = len(POOL_WINDOWS)
POOL_GROUP_DIM = D_MODEL // 8
POOL_DIM = N_POOL_GROUPS * POOL_GROUP_DIM

N_HEADS = D_MODEL // 128
QK_NOPE = 64
QK_ROPE = 32
V_DIM = 64
Q_LORA = 384
KV_LORA = 256
ATTN_DIM = N_HEADS * V_DIM

D_FF_2 = 4 * D_MODEL

N_MOD = 6

IN_SPLITS = (POOL_DIM, Q_LORA, KV_LORA, QK_ROPE, D_MODEL, D_MODEL)
D_IN_2 = sum(IN_SPLITS)


def rms_norm(x, g):
    xf = x.astype(jnp.float32)
    y = xf * lax.rsqrt(jnp.mean(xf * xf, axis=-1, keepdims=True) + EPS)
    return y.astype(x.dtype) * g

def apply_rope(x, cos, sin):
    half = x.shape[-1] // 2
    x1, x2 = x[..., :half], x[..., half:]
    return jnp.concatenate([x1 * cos - x2 * sin, x2 * cos + x1 * sin], axis=-1)

def pool_mixer(u, w_pool, pool_scale):
    B, S, _ = u.shape
    t = jnp.arange(S)
    outs = []
    for g, w in enumerate(POOL_WINDOWS):
        ug = u[..., g * POOL_GROUP_DIM:(g + 1) * POOL_GROUP_DIM].astype(jnp.float32)
        cs = jnp.cumsum(ug, axis=1)
        lag = jnp.pad(cs, ((0, 0), (w, 0), (0, 0)))[:, :S]
        cnt = jnp.minimum(t + 1, w).astype(jnp.float32)[None, :, None]
        outs.append(((cs - lag) / cnt - ug).astype(u.dtype))
    p = jnp.stack(outs, axis=2)
    y = jnp.einsum('bsgc,gcd->bsgd', p, w_pool).reshape(B, S, POOL_DIM)
    return y * pool_scale

def mla(c_q_raw, c_kv_raw, k_rope_raw, q_norm_g, w_uq, kv_norm_g, w_uk, w_uv, cos, sin):
    B, S, _ = c_q_raw.shape
    c_q = rms_norm(c_q_raw, q_norm_g)
    q = jnp.einsum('bsr,rhd->bshd', c_q, w_uq)
    q_nope = q[..., :QK_NOPE]
    q_rope = apply_rope(q[..., QK_NOPE:], cos[:, :, None, :], sin[:, :, None, :])
    c_kv = rms_norm(c_kv_raw, kv_norm_g)
    k_nope = jnp.einsum('bsr,rhd->bhsd', c_kv, w_uk)
    v = jnp.einsum('bsr,rhd->bhsd', c_kv, w_uv)
    k_rope = apply_rope(k_rope_raw, cos, sin)

    nb = S // Q_BLOCK
    def to_blocks(a):
        d = a.shape[-1]
        return a.reshape(B, nb, Q_BLOCK, N_HEADS, d).transpose(1, 0, 3, 2, 4)
    qn_b = to_blocks(q_nope)
    qr_b = to_blocks(q_rope)
    starts = jnp.arange(nb, dtype=jnp.int32) * Q_BLOCK
    key_pos = jnp.arange(S, dtype=jnp.int32)
    scale = 1.0 / math.sqrt(QK_NOPE + QK_ROPE)
    neg = jnp.finfo(jnp.float32).min

    def attend(args):
        qn, qr, start = args
        s = (jnp.einsum('bhqd,bhkd->bhqk', qn, k_nope)
             + jnp.einsum('bhqd,bkd->bhqk', qr, k_rope)).astype(jnp.float32) * scale
        q_pos = start + jnp.arange(Q_BLOCK, dtype=jnp.int32)
        mask = q_pos[:, None] >= key_pos[None, :]
        p = jax.nn.softmax(jnp.where(mask, s, neg), axis=-1)
        return jnp.einsum('bhqk,bhkd->bhqd', p.astype(v.dtype), v)

    o = lax.map(attend, (qn_b, qr_b, starts))
    return o.transpose(1, 0, 3, 2, 4).reshape(B, S, ATTN_DIM)

def second_inputs(seed: int = 0) -> dict:
    key = jax.random.key(seed)
    ks = jax.random.split(key, 24)
    f32 = jnp.float32

    def dense(k, shape, fan_in, mult=1.0):
        return jax.random.normal(k, shape, f32) * (mult * fan_in ** -0.5)

    def gain(k, shape):
        return 1.0 + 0.02 * jax.random.normal(k, shape, f32)

    x = jax.random.normal(ks[0], (BATCH, SEQ, D_MODEL), f32)
    c = jax.random.normal(ks[1], (BATCH, D_MODEL), f32)
    offsets = jax.random.randint(ks[2], (BATCH, 1), 0, 1024, dtype=jnp.int32)
    positions = offsets + jnp.arange(SEQ, dtype=jnp.int32)[None, :]
    return {
        "x": x,
        "c": c,
        "positions": positions,
        "ln1_g": gain(ks[3], (DEPTH, D_MODEL)),
        "ln2_g": gain(ks[4], (DEPTH, D_MODEL)),
        "w_ada": dense(ks[5], (DEPTH, D_MODEL, N_MOD * D_MODEL), D_MODEL, 0.5),
        "b_ada": 0.01 * jax.random.normal(ks[6], (DEPTH, N_MOD * D_MODEL), f32),
        "w_in": dense(ks[7], (DEPTH, D_MODEL, D_IN_2), D_MODEL),
        "q_norm_g": gain(ks[8], (DEPTH, Q_LORA)),
        "w_uq": dense(ks[9], (DEPTH, Q_LORA, N_HEADS, QK_NOPE + QK_ROPE), Q_LORA),
        "kv_norm_g": gain(ks[10], (DEPTH, KV_LORA)),
        "w_uk": dense(ks[11], (DEPTH, KV_LORA, N_HEADS, QK_NOPE), KV_LORA),
        "w_uv": dense(ks[12], (DEPTH, KV_LORA, N_HEADS, V_DIM), KV_LORA),
        "w_pool": dense(ks[13], (DEPTH, N_POOL_GROUPS, POOL_GROUP_DIM, POOL_GROUP_DIM), POOL_GROUP_DIM),
        "pool_scale": gain(ks[14], (DEPTH, POOL_DIM)),
        "p_pool": dense(ks[15], (DEPTH, POOL_DIM, D_MODEL), POOL_DIM),
        "p_attn": dense(ks[16], (DEPTH, ATTN_DIM, D_MODEL), ATTN_DIM),
        "w_out": dense(ks[17], (DEPTH, D_MODEL, D_MODEL), D_MODEL),
        "w_ff1": dense(ks[18], (DEPTH, D_MODEL, D_FF_2), D_MODEL),
        "w_ff2": dense(ks[19], (DEPTH, D_FF_2, D_MODEL), D_FF_2),
        "final_g": gain(ks[20], (D_MODEL,)),
    }

def second_block(x, c, positions, ln1_g, ln2_g, w_ada, b_ada, w_in, q_norm_g, w_uq,
              kv_norm_g, w_uk, w_uv, w_pool, pool_scale, p_pool, p_attn, w_out,
              w_ff1, w_ff2, final_g):
    inv_freq = ROPE_THETA ** (-jnp.arange(0, QK_ROPE, 2, dtype=jnp.float32) / QK_ROPE)
    ang = positions.astype(jnp.float32)[..., None] * inv_freq
    cos = jnp.cos(ang).astype(x.dtype)
    sin = jnp.sin(ang).astype(x.dtype)
    c_act = jax.nn.silu(c)
    cuts = np.cumsum(IN_SPLITS)[:-1].tolist()

    for l in range(DEPTH):
        mod = c_act @ w_ada[l] + b_ada[l]
        sh1, sc1, g1, sh2, sc2, g2 = [m[:, None, :] for m in jnp.split(mod, N_MOD, axis=-1)]

        h = rms_norm(x, ln1_g[l]) * (1.0 + sc1) + sh1
        z = h @ w_in[l]
        u_pool, c_q_raw, c_kv_raw, k_rope_raw, gz_a, gz_b = jnp.split(z, cuts, axis=-1)
        y_a = pool_mixer(u_pool, w_pool[l], pool_scale[l]) @ p_pool[l]
        y_b = mla(c_q_raw, c_kv_raw, k_rope_raw, q_norm_g[l], w_uq[l], kv_norm_g[l],
                  w_uk[l], w_uv[l], cos, sin) @ p_attn[l]
        merged = jax.nn.sigmoid(gz_a) * y_a + jax.nn.sigmoid(gz_b) * y_b
        x = x + g1 * (merged @ w_out[l])

        h2 = rms_norm(x, ln2_g[l]) * (1.0 + sc2) + sh2
        x = x + g2 * (jnp.square(jax.nn.relu(h2 @ w_ff1[l])) @ w_ff2[l])

    return rms_norm(x, final_g)


def setup_inputs(seed=0):
    out = dict(first_inputs(seed))
    for name, value in second_inputs(seed + 1).items():
        if name != "x":
            out[name + "_2"] = value
    return out


def reference(
    x, meta_tokens, norm_gains, ffn_w_gate, ffn_w_up, ffn_w_down, w_in, gla_w2, gla_b2, gla_gn,
    q_norm, k_norm, w_pa, w_pb, b_merge, w_out, final_norm, c_2, positions_2, ln1_g_2, ln2_g_2,
    w_ada_2, b_ada_2, w_in_2, q_norm_g_2, w_uq_2, kv_norm_g_2, w_uk_2, w_uv_2, w_pool_2,
    pool_scale_2, p_pool_2, p_attn_2, w_out_2, w_ff1_2, w_ff2_2, final_g_2,
):
    x = first_block(
        x, meta_tokens, norm_gains, ffn_w_gate, ffn_w_up, ffn_w_down, w_in, gla_w2, gla_b2,
        gla_gn, q_norm, k_norm, w_pa, w_pb, b_merge, w_out, final_norm,
    )
    return second_block(
        x, c_2, positions_2, ln1_g_2, ln2_g_2, w_ada_2, b_ada_2, w_in_2, q_norm_g_2, w_uq_2,
        kv_norm_g_2, w_uk_2, w_uv_2, w_pool_2, pool_scale_2, p_pool_2, p_attn_2, w_out_2,
        w_ff1_2, w_ff2_2, final_g_2,
    )


_drawn_inputs = setup_inputs


def setup_inputs(seed=0):
    import zlib

    import numpy as np

    out = dict(_drawn_inputs(seed))
    spreads = {}
    factors = {'gla_b2': 3.128,
     'gla_gn': 6.023,
     'q_norm': 8.0,
     'k_norm': 8.0,
     'b_merge': 8.0,
     'final_norm': 2.754,
     'ln1_g_2': 8.0,
     'ln2_g_2': 4.576,
     'b_ada_2': 2.669,
     'q_norm_g_2': 8.0,
     'kv_norm_g_2': 8.0,
     'pool_scale_2': 8.0,
     'final_g_2': 2.82}
    for name, (base, spread) in spreads.items():
        noise = np.random.default_rng([zlib.crc32(name.encode()), seed]).standard_normal(out[name].shape)
        drawn = base * np.exp(spread * noise) if base else spread * noise
        out[name] = __import__('jax').numpy.asarray(drawn.astype(out[name].dtype))
    for name, factor in factors.items():
        out[name] = (out[name] * factor).astype(out[name].dtype)
    return out
```

```python
from contextlib import ExitStack

import numpy as np

import concourse.bass as bass
from concourse import mybir

F32 = mybir.dt.float32
F32R = mybir.dt.float32r
I32 = mybir.dt.int32
ACT = mybir.ActivationFunctionType
ALU = mybir.AluOpType
AX = mybir.AxisListType.X

P = 128
L = 2
D = 1024
KD = D // P
META = 16
SEQ = 256
T = META + SEQ
EPS = 1e-6

FF = 2816
FG = FF // 256
KF = FF // P
GLA_H, GLA_DK, GLA_DV, CHUNK = 4, 64, 128, 64
TILES = [(0, META), (META, P), (META + P, P)]
CHUNKS = [(0, 0, META)] + [(1 + i // 2, 64 * (i % 2), CHUNK) for i in range(4)]
CHUNK_COL = [0, 16, 80, 144, 208]
AH, HD = 8, 64

FF2 = 4096
KF2 = FF2 // P
MH, NOPE, ROPE, VD = 8, 64, 32, 64
QK = NOPE + ROPE
QL, KVL = 384, 256
POOL_W = (2, 4, 8, 16)
N_MOD = 6

GU_W, DN_W = 2048, 2816
FFN_W = FG * 2 * GU_W + 4 * 2 * DN_W
MIX1 = 25
W1_FFN = [0, FFN_W + MIX1 * 2048]
W1_MIX = FFN_W
W1_ALL = 2 * FFN_W + MIX1 * 2048
M2_WIDTH = [2048, 2048, 1280, 2048, 2048, 2304, 2048] + [2048] * 8 + [512] + [2048] * 8
M2_OFF = [sum(M2_WIDTH[:i]) for i in range(len(M2_WIDTH) + 1)]
W2_FF1 = M2_OFF[-1]
W2_FF2 = W2_FF1 + 16 * 2048
W2_ALL = W2_FF2 + 16 * 2048
ADA_N = N_MOD * D
RAW_W, UNIT_W = 2816, 1408

C_ID, C_ONE, C_BLK = 0, 128, 256
C_CUM, C_END = [384, 512], [640, 768]
C_ROT, C_DUP = 896, [1024, 1152]
C_DROT = [1280, 1408]
C_COS, C_SIN = 1536, 1536 + T
C_R32 = C_SIN + T
C_INV = C_R32 + 32
C_MASK = C_INV + 1
C_CNT = C_MASK + 384
C_EPS = C_CNT + 64
C_ALL = C_EPS + 1

V_GAIN, V_BM, V_GN, V_QN, V_KN, V1_ALL = 0, 24, 40, 44, 45, 46
V_LN1, V_LN2, V_QG, V_KVG, V_PS, V2_ALL = 0, 8, 16, 19, 21, 25
G_FN, G_FG, G_C, G_ALL = 0, 8, 16, 24


class Event:

    def __init__(self, line, value):
        self.line, self.value = line, value


class Counts:

    def __init__(self, nc, ctx):
        self.nc = nc
        self.engine = {"pe": nc.tensor, "act": nc.scalar, "dve": nc.vector, "pool": nc.gpsimd, "sp": nc.sync}
        lines = ["pe", "act", "dve", "pool", "rawA", "rawB", "small", "vec", "ada"]
        self.sem = {n: ctx.enter_context(nc.semaphore(f"{n}_done")) for n in lines}
        self.out_sem = ctx.enter_context(nc.semaphore("out_done"))
        self.layer = 0
        self.kept = {}
        self.reset()

    def reset(self):
        self.count = {n: 0 for n in self.sem}
        self.seen = {}
        self.loop = None
        self.made = []

    def done(self, line, ins, by=1):
        ins.then_inc(self.sem[line], by)
        self.count[line] += by
        e = Event(line, self.count[line])
        self.made.append(e)
        return e

    def need(self, engine, *events):
        want = {}
        for e in events:
            if e is None:
                continue
            if isinstance(e, (list, tuple)):
                for x in e:
                    if x is not None:
                        want[x.line] = max(want.get(x.line, 0), x.value)
            else:
                want[e.line] = max(want.get(e.line, 0), e.value)
        for line, value in want.items():
            if self.seen.get((engine, line), 0) >= value:
                continue
            self.seen[engine, line] = value
            if self.loop and value > self.loop["base"][line]:
                value = value + self.loop["reg"] * self.loop["stride"][line]
            if line in self.kept:
                value = value + self.layer * self.kept[line]
            self.engine[engine].wait_ge(self.sem[line], value)

    def repeat(self, n, body):
        base = dict(self.count)
        body(0)
        mid = dict(self.count)
        stride = {k: mid[k] - base[k] for k in mid}
        self.made = []
        with self.nc.Fori(0, n - 2) as reg:
            self.loop = {"base": base, "stride": stride, "reg": reg}
            self.seen = {}
            body(reg + 1)
            assert all(self.count[k] - mid[k] == stride[k] for k in mid)
        self.loop = None
        self.seen = {}
        for e in self.made:
            e.value += (n - 3) * stride[e.line]
        for k in self.count:
            self.count[k] += (n - 3) * stride[k]
        body(n - 1)

    def new_layer(self):
        self.nc.all_engine_barrier()
        for n in self.sem:
            if n not in self.kept:
                self.nc.gpsimd.sem_clear(self.sem[n])
        self.nc.all_engine_barrier()
        self.reset()


def program(nc, x0, w1, w2cat, lr_w, vec1, w2, vec2, vecg, ada_w, b_ada, pos, const, masks, out):
    with ExitStack() as ctx:
        place = [nc.sbuf_base, nc.sbuf_top]

        def sb(name, shape, dt=F32):
            at = (place[0] + 63) // 64 * 64
            place[0] = at + 4 * int(np.prod(shape[1:]))
            assert place[0] <= place[1], (name, place)
            return nc.alloc_sbuf_tensor_at(name, shape, dt, offset=at)

        ct = Counts(nc, ctx)
        done, need = ct.done, ct.need
        pe, act, dve, pool, sp = nc.tensor, nc.scalar, nc.vector, nc.gpsimd, nc.sync
        bank = [ctx.enter_context(nc.psum_tensor(f"bank{i}", [P, 512], F32)) for i in range(8)]
        bank_free = [None] * 8

        x = sb("x", [P, KD, T])
        xn_hi = sb("xn_hi", [P, KD, T], F32R)
        xn_lo = sb("xn_lo", [P, KD, T], F32R)
        sumsq = sb("sumsq", [P, T])
        sq = sb("sq", [P, T])
        sq2 = sb("sq2", [P, T])
        rstd = sb("rstd", [P, T])
        full = sb("full", [P, 2, T])
        gate = sb("gate", [P, 2, T])
        raw = [sb("rawA", [P, RAW_W]), sb("rawB", [P, RAW_W])]
        w_hi = [sb(f"w_hi{u}", [P, UNIT_W], F32R) for u in range(4)]
        w_lo = [sb(f"w_lo{u}", [P, UNIT_W], F32R) for u in range(4)]
        cst = sb("cst", [P, C_ALL])
        vg = sb("vg", [P, G_ALL])
        c_act = sb("c_act", [P, KD])
        mod_all = sb("mod_all", [P, L, 48])

        ident = cst[:, C_ID:C_ID + P]
        ones = cst[:, C_ONE:C_ONE + P]
        eps = cst[:, C_EPS:C_EPS + 1]

        def A(ins):
            return done("act", ins)

        def V(ins):
            return done("dve", ins)

        def M(ins):
            return done("pe", ins)

        def G(ins):
            return done("pool", ins)

        def evacuated(b, *events):
            bank_free[b] = list(events)

        class Stream:
            landed = [None, None]
            split_of = [None] * 4
            unit_free = [None] * 4
            raw_users = [[], []]

        S = Stream()

        def load(slot, src):
            need("sp", S.raw_users[slot])
            S.raw_users[slot] = []
            w = src.shape[1]
            S.landed[slot] = done(("rawA", "rawB")[slot], sp.dma_start(raw[slot][:, 0:w], src), 16)

        def split(pair, u):
            if pair is None or pair.width[u] == 0:
                return
            slot, w = u // 2, pair.width[u]
            at = pair.width[2 * slot] if u % 2 else 0
            src = raw[slot][:, at:at + w]
            need("act", S.landed[slot], S.unit_free[u])
            a = A(act.activation(w_hi[u][:, 0:w], src, ACT.Copy))
            need("dve", S.landed[slot], S.unit_free[u], a)
            v = V(dve.tensor_tensor(w_lo[u][:, 0:w], src, w_hi[u][:, 0:w].bitcast(F32), ALU.subtract))
            S.split_of[u] = [a, v]
            S.raw_users[slot] += [v]

        class Pair:

            def __init__(self, src, width, work, post):
                self.src, self.width, self.work, self.post = src, width, work, post

        def load_pair(pair):
            for slot in (0, 1):
                if pair.src[slot] is not None:
                    load(slot, pair.src[slot])

        def start(pair):
            load_pair(pair)
            for u in range(3):
                split(pair, u)

        def finish(chains):
            for g in chains:
                for _ in g:
                    pass

        def run_pair(cur, nxt, side=(), extra=None, stop_side=None):
            split(cur, 3)
            if nxt is not None:
                load_pair(nxt)
            for u in range(4):
                if u:
                    split(nxt, u - 1)
                if u == stop_side:
                    finish(side)
                if cur.work[u] is not None:
                    need("pe", S.split_of[u])
                    w = cur.width[u]
                    S.unit_free[u] = M(cur.work[u](w_hi[u][:, 0:w], w_lo[u][:, 0:w]))
                    if cur.post[u] is not None:
                        cur.post[u](S.unit_free[u])
                if extra is not None and u == 2:
                    extra()
                for g in side:
                    next(g, None)

        def product(o, wh, wl, xh, xl, first, last):
            pe.matmul(o, wh, xh, start=first, stop=False)
            pe.matmul(o, wh, xl, start=False, stop=False)
            return pe.matmul(o, wl, xh, start=False, stop=last)

        def inverse_root(dst, src, scale, *waits):
            n = dst.shape[0]
            need("act", *waits)
            e = A(act.activation(dst, src, ACT.Ln, bias=eps[dst_rows(dst)], scale=scale))
            need("act", e)
            return A(act.activation(dst, dst, ACT.Exp, scale=-0.5))

        def dst_rows(dst):
            return slice(0, dst.shape[0])

        sq_free = [None, None]
        sumsq_free = [None]
        xn_ready = [None] * KD
        xn_free = [None]
        full_free = [[], []]

        def normalise(cols, gain, bias=None, b=7, into=None):
            need("pe", sumsq_free[0], bank_free[b])
            n = cols.stop - cols.start
            m = M(pe.matmul(bank[b][:, 0:n], ones, sumsq[:, cols], start=True, stop=True))
            r = inverse_root(rstd[:, cols], bank[b][:, 0:n], 1.0 / D, m)
            evacuated(b, r)
            sumsq_free[0] = m
            lo_cols = slice(0, n)
            for k in range(KD):
                j = k % 2
                need("dve", r, full_free[j])
                t = V(dve.tensor_tensor(full[:, j, 0:n], x[:, k, cols], rstd[:, cols], ALU.mult))
                if into is not None:
                    need("dve", t)
                    full_free[j] = [V(dve.tensor_scalar(x[:, k, cols], full[:, j, 0:n], gain[:, k:k + 1], None, ALU.mult))]
                    into.append(full_free[j][0])
                    continue
                need("act", t, xn_free[0])
                if bias is None:
                    a = A(act.activation(xn_hi[:, k, lo_cols], full[:, j, 0:n], ACT.Copy, scale=gain[:, k:k + 1]))
                    need("dve", a, xn_free[0])
                    v = V(dve.scalar_tensor_tensor(out=xn_lo[:, k, lo_cols], in0=full[:, j, 0:n], scalar=gain[:, k:k + 1],
                                                   in1=xn_hi[:, k, lo_cols].bitcast(F32), op0=ALU.mult, op1=ALU.subtract))
                else:
                    need("dve", t)
                    t = V(dve.tensor_scalar(full[:, j, 0:n], full[:, j, 0:n], gain[:, k:k + 1], bias[:, k:k + 1], ALU.mult, ALU.add))
                    need("act", t)
                    a = A(act.activation(xn_hi[:, k, lo_cols], full[:, j, 0:n], ACT.Copy))
                    need("dve", a)
                    v = V(dve.tensor_tensor(xn_lo[:, k, lo_cols], full[:, j, 0:n], xn_hi[:, k, lo_cols].bitcast(F32), ALU.subtract))
                full_free[j] = [a, v]
                xn_ready[k] = [a, v]

        def split_rows(hi, lo, src, *waits):
            need("act", *waits)
            a = A(act.activation(hi, src, ACT.Copy))
            need("dve", a, *waits)
            v = V(dve.tensor_tensor(lo, src, hi.bitcast(F32), ALU.subtract))
            return [a, v]

        def feature_tile(b, rows, n, k_tiles, xh, xl, ready, col=0, step=P, off=0, ps_rows=None):
            def work(wh, wl):
                need("pe", bank_free[b])
                for k in range(k_tiles):
                    need("pe", ready[k])
                    s = slice(off + k * step + col, off + k * step + col + rows)
                    o = bank[b][0:rows, 0:n] if ps_rows is None else bank[b][ps_rows, 0:n]
                    m = product(o, wh[:, s], wl[:, s], xh[:, k, 0:n], xl[:, k, 0:n], k == 0, k == k_tiles - 1)
                return m
            return work

        e_const = done("small", sp.dma_start(cst[:, :], const), 16)
        e_const = done("small", sp.dma_start(vg[:, :], vecg), 16)
        e_x = done("small", sp.dma_start(x[:, :, :], x0.rearrange("p (k t) -> p k t", k=KD)), 16)
        need("act", e_x)
        A(act.activation(c_act[:, :], vg[:, G_C:G_C + KD], ACT.Silu))
        need("act", Event("act", ct.count["act"]))
        ct.new_layer()

        TA = slice(0, T)
        if True:
            block_start = place[0]
            v1 = sb("v1", [P, V1_ALL])
            bada = sb("bada", [P, 48])
            att = [sb(f"att{i}", [P, T]) for i in range(4)]
            msk = sb("msk", [P, 2, T], I32)
            shared_start = place[0]
            h_hi = sb("h_hi", [P, KF, T], F32R)
            h_lo = sb("h_lo", [P, KF, T], F32R)
            acc = sb("acc", [P, ADA_N])
            ada_raw = sb("ada_raw", [P, 2048])
            place[0] = shared_start
            qa = sb("qa", [P, 2, T])
            ka = sb("ka", [P, 2, T])
            vtok = sb("vtok", [P, 3, 512])
            r_act = sb("r_act", [P, 4, T])
            qb = sb("qb", [P, 4, T])
            kb = sb("kb", [P, T])
            kdup = sb("kdup", [P, 2, T])
            vb = sb("vb", [P, 3, P])
            qdec = sb("qdec", [P, 4, T])
            kinv = sb("kinv", [P, 4, T])
            states = sb("states", [P, 4, 4, P])
            decay = sb("decay", [P, 4, 5])
            gates = sb("gates", [P, 16, T])
            b_hi = sb("b_hi", [P, 4, T], F32R)
            b_lo = sb("b_lo", [P, 4, T], F32R)
            stat = sb("stat", [P, 16])
            qb_meta = sb("qb_meta", [P, 4, META])
            reused = place[0]
            la = sb("la", [P, 3, 512])
            e_cum = sb("e_cum", [P, 2, T])
            kend_t = sb("kend_t", [P, 2, 3, P])
            end_la = place[0]
            place[0] = reused
            a_hi = sb("a_hi", [P, 4, T], F32R)
            a_lo = sb("a_lo", [P, 4, T], F32R)
            place[0] = reused = max(place[0], end_la)
            lr_raw = sb("lr_raw", [P, 256])
            lr_hi = sb("lr_hi", [P, 256], F32R)
            lr_lo = sb("lr_lo", [P, 256], F32R)
            w2c = sb("w2c", [33, 512])
            lrT = sb("lrT", [33, T])
            place[0] = reused
            prob = sb("prob", [P, 2, T])
            pt = sb("pt", [P, 2, 3, SEQ])
            lt = sb("lt", [P, 3, P])
            y_hi, y_lo = xn_hi, xn_lo

            for a4 in att:
                z = G(pool.memset(a4[:, :], 0.0))
            e_mask = done("small", sp.dma_start(msk[:, :, :], masks.rearrange("p (d t) -> p d t", d=2)), 16)
            need("dve", z, e_mask)
            need("pool", e_mask)
            ct.new_layer()

            def layer1(l):
                for i in range(8):
                    bank_free[i] = None
                S.landed, S.split_of, S.unit_free, S.raw_users = [None] * 2, [None] * 4, [None] * 4, [[], []]
                sq_free[0] = sq_free[1] = sumsq_free[0] = xn_free[0] = None
                full_free[0], full_free[1] = [], []
                small = done("vec", act.dma_start(v1[:, :], vec1[l]), 16)
                small = done("vec", act.dma_start(bada[:, :], b_ada[l]), 16)
                ada = {"landed": None, "used": None}

                def ada_load(f, j):
                    need("pool", ada["used"])
                    ada["landed"] = done("ada", pool.dma_start(
                        ada_raw[:, :], ada_w[l, :, bass.ds((f * 12 + j) * 2048, 2048)] if not isinstance(j, int)
                        else ada_w[l, :, (f * 12 + j) * 2048:(f * 12 + j + 1) * 2048]), 16)

                def ada_piece(f, j):
                    o = acc[:, bass.ds(j * 512, 512)]
                    need("dve", ada["landed"])
                    for i in range(4):
                        w, c = ada_raw[:, i * 512:(i + 1) * 512], c_act[:, 4 * f + i:4 * f + i + 1]
                        if i == 0:
                            v = V(dve.tensor_scalar(o, w, c, None, ALU.mult))
                        else:
                            v = V(dve.scalar_tensor_tensor(out=o, in0=w, scalar=c, in1=o, op0=ALU.mult, op1=ALU.add))
                        need("dve", v)
                    ada["used"] = v

                def w1_src(off, w, step=0, i=0):
                    o = off + i * step
                    return w1[l, :, bass.ds(o, w)]

                h_ready = [None] * KF
                gate_free = [None, None]

                def gate_up(f, i):
                    o = W1_FFN[f]
                    src = [w1_src(o, GU_W, 2 * GU_W, i), w1_src(o + GU_W, GU_W, 2 * GU_W, i)]
                    work = [feature_tile(b, P, T, KD, xn_hi, xn_lo, xn_ready) for b in range(4)]

                    def gated(j):
                        def post(m):
                            need("act", m, gate_free[j])
                            g = A(act.activation(gate[:, j, :], bank[j][:, 0:T], ACT.Silu))
                            evacuated(j, g)
                            need("dve", m, g, full_free[j])
                            v = V(dve.tensor_tensor(full[:, j, :], gate[:, j, :], bank[2 + j][:, 0:T], ALU.mult))
                            gate_free[j] = v
                            evacuated(2 + j, v)
                            hh, hl = h_hi[:, bass.ds(2 * i + j, 1), :], h_lo[:, bass.ds(2 * i + j, 1), :]
                            fj = full[:, j:j + 1, :]
                            need("act", v)
                            a = A(act.activation(hh, fj, ACT.Copy))
                            need("dve", a)
                            v = V(dve.tensor_tensor(hl, fj, hh.bitcast(F32), ALU.subtract))
                            full_free[j] = [a, v]
                            h_last[0] = [a, v]
                        return post
                    return Pair(src, [1024] * 4, work, [None, None, gated(0), gated(1)])

                h_last = [None]
                HK = KF // 2

                def down(f, g):
                    o = W1_FFN[f] + FG * 2 * GU_W
                    src = [w1_src(o, DN_W, 2 * DN_W, g), w1_src(o + DN_W, DN_W, 2 * DN_W, g)]

                    def part(half, j):
                        def work(wh, wl):
                            b = 4 + j
                            if half == 0:
                                need("pe", bank_free[b])
                            need("pe", h_last[0])
                            for k in range(HK):
                                s = slice(k * P, (k + 1) * P)
                                kk = half * HK + k
                                m = product(bank[b][:, 0:T], wh[:, s], wl[:, s], h_hi[:, kk, :], h_lo[:, kk, :],
                                            kk == 0, kk == KF - 1)
                            return m
                        return work

                    def add(j):
                        def post(m):
                            xk = x[:, bass.ds(2 * g + j, 1), :]
                            need("dve", m)
                            v = V(dve.scalar_tensor_tensor(out=xk, in0=bank[4 + j][:, 0:T].rearrange("p (a t) -> p a t", a=1),
                                                           scalar=0.5, in1=xk, op0=ALU.mult, op1=ALU.add))
                            evacuated(4 + j, v)
                            sum_squares_of(xk, v)
                        return post
                    return Pair(src, [1408] * 4, [part(0, 0), part(0, 1), part(1, 0), part(1, 1)], [None, None, add(0), add(1)])

                def sum_squares_of(xk, ev):
                    need("dve", ev, sq_free[0])
                    v = V(dve.tensor_tensor(sq[:, :], xk.rearrange("p a t -> p (a t)") if len(xk.shape) == 3 else xk, xk.rearrange("p a t -> p (a t)") if len(xk.shape) == 3 else xk, ALU.mult))
                    need("dve", v, sumsq_free[0])
                    v = V(dve.tensor_tensor(sumsq[:, :], sumsq[:, :], sq[:, :], ALU.add))
                    sq_free[0] = sumsq_free[0] = v

                def clear_sumsq():
                    need("dve", sumsq_free[0])
                    sumsq_free[0] = V(dve.memset(sumsq[:, :], 0.0))

                def ffn(f, gain, nxt):
                    normalise(TA, gain)
                    clear_sumsq()
                    ada_load(f, 0)

                    def step(i):
                        last = isinstance(i, int) and i == FG - 1

                        def extra():
                            ada_piece(f, i)
                            ada_load(f, i + 1)
                        run_pair(gate_up(f, i), down(f, 0) if last else gate_up(f, i + 1), extra=extra)
                    ct.repeat(FG, step)
                    xn_free[0] = S.unit_free[3]

                    def dstep(g):
                        last = isinstance(g, int) and g == 3
                        run_pair(down(f, g), nxt if last else down(f, g + 1))
                    ada_piece(f, 11)
                    ct.repeat(4, dstep)

                a_ready, b_ready, y_ready = [None] * 4, [None] * 4, [None] * KD

                def mix_src(c):
                    return w1_src(W1_MIX + 2048 * c, 2048)

                ev = {}

                def copy_to(dst, b, key, scale=1.0, bias=None):
                    def post(m):
                        need("act", m)
                        if bias is None:
                            e = A(act.activation(dst, bank[b][:, 0:T], ACT.Copy, scale=scale))
                        else:
                            e = A(act.activation(dst, bank[b][:, 0:T], ACT.Identity, bias=bias))
                        ev[key] = e
                        evacuated(b, e)
                    return post

                def xtile(b):
                    return feature_tile(b, P, T, KD, xn_hi, xn_lo, xn_ready)

                def token_tiles(bs, cols, width=P):
                    def work(wh, wl):
                        for t, (c0, n) in enumerate(TILES):
                            b = bs[t]
                            need("pe", bank_free[b])
                            o = bank[b][0:n, cols[t]:cols[t] + width]
                            for k in range(KD):
                                need("pe", xn_ready[k])
                                s = slice(k * width, (k + 1) * width)
                                cs = slice(c0, c0 + n)
                                pe.matmul(o, xn_hi[:, k, cs], wh[:, s], start=k == 0, stop=False)
                                pe.matmul(o, xn_lo[:, k, cs], wh[:, s], start=False, stop=False)
                                m = pe.matmul(o, xn_hi[:, k, cs], wl[:, s], start=False, stop=k == KD - 1)
                        return m
                    return work

                def v_out(m):
                    need("act", m)
                    for t, (c0, n) in enumerate(TILES):
                        e = A(act.activation(vtok[0:n, t, :], bank[4 + t][0:n, :], ACT.Copy))
                        evacuated(4 + t, e)
                    ev["v"] = e

                def vb_out(m):
                    need("act", m)
                    for t, (c0, n) in enumerate(TILES):
                        e = A(act.activation(vb[0:n, t, :], bank[1][0:n, t * P:(t + 1) * P], ACT.Copy))
                    evacuated(1, e)
                    ev["vb"] = e

                def gate_out(j, b):
                    return copy_to(gates[:, j, :], b, ("g", j), bias=v1[:, V_BM + j:V_BM + j + 1])

                def log_gates():
                    w = done("vec", act.dma_start(lr_raw[:, :], lr_w[l]), 16)
                    w = done("vec", act.dma_start(w2c[:, :], w2cat[l]), 16)
                    s = split_rows(lr_hi[:, :], lr_lo[:, :], lr_raw[:, :], w)
                    need("dve")
                    one = V(dve.memset(lrT[32:33, :], 1.0))
                    need("pe", s, bank_free[4])
                    for k in range(KD):
                        need("pe", xn_ready[k])
                        ks = slice(32 * k, 32 * k + 32)
                        m = product(bank[4][0:32, 0:T], lr_hi[:, ks], lr_lo[:, ks], xn_hi[:, k, :], xn_lo[:, k, :], k == 0, k == KD - 1)
                    m = M(m)
                    need("act", m)
                    e = A(act.activation(lrT[0:32, :], bank[4][0:32, 0:T], ACT.Copy))
                    evacuated(4, e)
                    need("pe", e, one)
                    for t, (c0, n) in enumerate(TILES):
                        need("pe", bank_free[5 + t])
                        m = M(pe.matmul(bank[5 + t][0:n, :], lrT[0:33, c0:c0 + n], w2c[0:33, :], start=True, stop=True))
                        need("act", m)
                        e = A(act.activation(la[0:n, t, :], bank[5 + t][0:n, :], ACT.Abs))
                        need("act", e)
                        e = A(act.activation(la[0:n, t, :], la[0:n, t, :], ACT.Exp, scale=-1.0))
                        need("act", e)
                        e = A(act.activation(la[0:n, t, :], la[0:n, t, :], ACT.Ln, bias=ones[0:n, 0:1]))
                        need("dve", e)
                        v = V(dve.scalar_tensor_tensor(out=la[0:n, t, :], in0=bank[5 + t][0:n, :], scalar=0.0, in1=la[0:n, t, :],
                                                       op0=ALU.min, op1=ALU.subtract))
                        evacuated(5 + t, v)
                    ev["la"] = v

                def gla():
                    kt_free = [None, None]
                    e_free = [None, None]
                    for d in range(2):
                        for p in range(2):
                            i = 2 * d + p
                            need("pe", ev["la"])
                            for b, c in ((2, C_CUM[d]), (3, C_END[d])):
                                need("pe", bank_free[b])
                                for t, (c0, n) in enumerate(TILES):
                                    m = pe.matmul(bank[b][:, c0:c0 + n], la[0:n, t, d * 256 + p * P:d * 256 + p * P + P],
                                                  cst[0:n, c:c + n], start=True, stop=True)
                            m = M(m)
                            need("act", m, e_free[0], e_free[1])
                            e0 = A(act.activation(e_cum[:, 0, :], bank[2][:, 0:T], ACT.Exp))
                            e1 = A(act.activation(e_cum[:, 1, :], bank[2][:, 0:T], ACT.Exp, scale=-1.0))
                            evacuated(2, e1)
                            need("dve", e0, ev["qa", p])
                            V(dve.tensor_tensor(qdec[:, i, :], qa[:, p, :], e_cum[:, 0, :], ALU.mult))
                            for c in range(5):
                                cc = CHUNK_COL[c] + (CHUNKS[c][2] - 1 if d == 0 else 0)
                                v = V(dve.tensor_copy(decay[:, i, c:c + 1], e_cum[:, 0, cc:cc + 1]))
                            need("dve", e1, ev["ka", p])
                            v = V(dve.tensor_tensor(kinv[:, i, :], ka[:, p, :], e_cum[:, 1, :], ALU.mult))
                            need("act", v)
                            e2 = A(act.activation(e_cum[:, 0, :], bank[3][:, 0:T], ACT.Exp))
                            evacuated(3, e2)
                            need("dve", e2)
                            v = V(dve.tensor_tensor(e_cum[:, 1, :], ka[:, p, :], e_cum[:, 0, :], ALU.mult))
                            e_free[0] = v
                            yield
                            need("pe", v, bank_free[4])
                            for t, (c0, n) in enumerate(TILES):
                                m = pe.transpose(bank[4][0:n, t * P:(t + 1) * P], e_cum[:, 1, c0:c0 + n], ident)
                            m = M(m)
                            e_free[1] = m
                            j = i % 2
                            need("act", m, kt_free[j])
                            A(act.activation(kend_t[0:META, j, 0, :], bank[4][0:META, 0:P], ACT.Copy))
                            e = A(act.activation(kend_t[:, j, 1:3, :], bank[4][:, P:3 * P], ACT.Copy))
                            evacuated(4, e)
                            yield
                            need("pe", e, ev["v"], bank_free[2], bank_free[3])
                            order = [0, 1, 2, 3] if d == 0 else [4, 3, 2, 1]
                            for s, c in enumerate(order):
                                t, po, n = CHUNKS[c]
                                for hh in range(2):
                                    h = 2 * p + hh
                                    m = pe.matmul(bank[3 if po else 2][64 * hh:64 * hh + 64, s * P:(s + 1) * P],
                                                  kend_t[po:po + n, j, t, 64 * hh:64 * hh + 64],
                                                  vtok[po:po + n, t, h * P:(h + 1) * P], start=True, stop=True)
                            m = M(m)
                            kt_free[j] = m
                            need("dve", m)
                            v = V(dve.tensor_copy(states[:, i, 0, :], bank[3 if CHUNKS[order[0]][1] else 2][:, 0:P]))
                            for s in range(1, 4):
                                need("dve", v)
                                v = V(dve.scalar_tensor_tensor(out=states[:, i, s, :], in0=states[:, i, s - 1, :],
                                                               scalar=decay[:, i, order[s]:order[s] + 1],
                                                               in1=bank[3 if CHUNKS[order[s]][1] else 2][:, s * P:(s + 1) * P],
                                                               op0=ALU.mult, op1=ALU.add))
                            evacuated(2, v)
                            evacuated(3, v)
                            ev["state", i] = v
                            yield
                    att_free = [None] * 4
                    for h in range(GLA_H):
                        p, hr = h // 2, slice(64 * (h % 2), 64 * (h % 2) + 64)
                        for d in range(2):
                            i, b, o = 2 * d + p, 2 + d, att[2 * (h % 2) + d]
                            need("pe", ev["state", i], bank_free[b])
                            for t, (c0, n) in enumerate(TILES):
                                m = pe.matmul(bank[b][0:n, c0:c0 + n], kinv[hr, i, c0:c0 + n], qdec[hr, i, c0:c0 + n],
                                              start=True, stop=True)
                            m = M(m)
                            need("dve", m, att_free[2 * (h % 2) + d])
                            V(dve.copy_predicated(o[0:META, 0:META], msk[0:META, d, 0:META], bank[b][0:META, 0:META]))
                            v = V(dve.copy_predicated(o[:, META:T], msk[:, d, META:T], bank[b][:, META:T]))
                            evacuated(b, v)
                        yield
                        need("pe", v, bank_free[4])
                        for t, (c0, n) in enumerate(TILES):
                            vt = vtok[0:n, t, h * P:(h + 1) * P]
                            todo = []
                            for d in range(2):
                                i = 2 * d + p
                                todo.append((bank[4][:, c0:c0 + n], vt, att[2 * (h % 2) + d][0:n, c0:c0 + n]))
                                order = [0, 1, 2, 3] if d == 0 else [4, 3, 2, 1]
                                for s, c in enumerate([1, 2, 3, 4] if d == 0 else [3, 2, 1, 0]):
                                    if CHUNKS[c][0] == t:
                                        cs = slice(CHUNK_COL[c], CHUNK_COL[c] + CHUNKS[c][2])
                                        todo.append((bank[4][:, cs], states[hr, i, s, :], qdec[hr, i, cs]))
                            todo.sort(key=lambda z: z[2].shape[0] != n)
                            for q, (o, lh, rh) in enumerate(todo):
                                m = pe.matmul(o, lh, rh, start=q == 0, stop=q == len(todo) - 1, skip_group_check=True)
                        m = M(m)
                        att_free[2 * (h % 2)] = att_free[2 * (h % 2) + 1] = m
                        need("act", m, sq_free[0])
                        a = A(act.activation(sq[:, :], bank[4][:, 0:T], ACT.Square))
                        need("pe", a, bank_free[2])
                        m2 = M(pe.matmul(bank[2][:, 0:T], ones, sq[:, :], start=True, stop=True))
                        sq_free[0] = m2
                        yield
                        r = inverse_root(gate[:, 0, :], bank[2][:, 0:T], 1.0 / GLA_DV, m2, gate_free[0])
                        evacuated(2, r)
                        need("dve", r, full_free[0])
                        v = V(dve.tensor_tensor(full[:, 0, :], bank[4][:, 0:T], gate[:, 0, :], ALU.mult))
                        gate_free[0] = v
                        evacuated(4, v)
                        need("dve", v, ev["silu_r"])
                        v = V(dve.scalar_tensor_tensor(out=full[:, 0, :], in0=full[:, 0, :], scalar=v1[:, V_GN + h:V_GN + h + 1],
                                                       in1=r_act[:, h, :], op0=ALU.mult, op1=ALU.mult))
                        a_ready[h] = split_rows(a_hi[:, h, :], a_lo[:, h, :], full[:, 0, :], v)
                        full_free[0] = a_ready[h]
                        yield

                def attention():
                    for k in range(5):
                        src = qb[:, k, :] if k < 4 else kb[:, :]
                        need("act", sq_free[1], ev["qb", k] if k < 4 else ev["kb"], ev["la"])
                        a = A(act.activation(sq2[:, :], src, ACT.Square))
                        need("pe", a, bank_free[ATB[0]])
                        b = ATB[0]
                        m = M(pe.matmul(bank[b][:, 0:T], cst[:, C_BLK:C_BLK + P], sq2[:, :], start=True, stop=True))
                        sq_free[1] = m
                        r = inverse_root(gate[:, 1, :], bank[b][:, 0:T], 1.0 / HD, m, gate_free[1])
                        evacuated(b, r)
                        need("dve", r)
                        g = V_QN if k < 4 else V_KN
                        v = V(dve.scalar_tensor_tensor(out=src, in0=src, scalar=v1[:, g:g + 1], in1=gate[:, 1, :],
                                                       op0=ALU.mult, op1=ALU.mult))
                        gate_free[1] = v
                        yield
                        b = ATB[0]
                        if k < 4:
                            need("pe", v, bank_free[b])
                            m = M(pe.matmul(bank[b][:, 0:T], cst[:, C_ROT:C_ROT + P], src, start=True, stop=True))
                            need("dve", m, full_free[1])
                            v = V(dve.tensor_tensor(full[:, 1, :], bank[b][:, 0:T], cst[:, C_SIN:C_SIN + T], ALU.mult))
                            evacuated(b, v)
                            v2 = V(dve.tensor_tensor(src, src, cst[:, C_COS:C_COS + T], ALU.mult))
                            need("dve", v2)
                            v = V(dve.tensor_tensor(src, src, full[:, 1, :], ALU.add))
                            full_free[1] = [v]
                            need("dve", v)
                            V(dve.tensor_copy(qb_meta[:, k, :], qb[:, k, 0:META]))
                        else:
                            for g in range(2):
                                b2 = ATB[1]
                                need("pe", v, bank_free[b], bank_free[b2])
                                pe.matmul(bank[b][:, 0:T], cst[:, C_DROT[g]:C_DROT[g] + P], src, start=True, stop=True)
                                m = M(pe.matmul(bank[b2][:, 0:T], cst[:, C_DUP[g]:C_DUP[g] + P], src, start=True, stop=True))
                                need("dve", m, full_free[1])
                                v3 = V(dve.tensor_tensor(full[:, 1, :], bank[b][:, 0:T], cst[:, C_SIN:C_SIN + T], ALU.mult))
                                evacuated(b, v3)
                                v2 = V(dve.tensor_tensor(kdup[:, g, :], bank[b2][:, 0:T], cst[:, C_COS:C_COS + T], ALU.mult))
                                evacuated(b2, v2)
                                need("dve", v2)
                                v3 = V(dve.tensor_tensor(kdup[:, g, :], kdup[:, g, :], full[:, 1, :], ALU.add))
                                full_free[1] = [v3]
                            v = v3
                        ev["rope"] = v
                        yield
                    prob_free = [None, None]
                    st = [0]

                    def softmax(b, j):
                        c = 4 * (st[0] % 4)
                        st[0] += 1
                        mx, nb, su, rc = (stat[:, c + i:c + i + 1] for i in range(4))
                        v = V(dve.reduce_max(mx, bank[b][:, 0:T], AX))
                        need("dve", v)
                        v = V(dve.tensor_scalar(nb, mx, -HD ** -0.5, None, ALU.mult))
                        need("act", v, prob_free[j])
                        a = A(act.activation(prob[:, j, :], bank[b][:, 0:T], ACT.Exp, bias=nb, scale=HD ** -0.5, accum_out=su))
                        evacuated(b, a)
                        need("dve", a)
                        v = V(dve.reciprocal(rc, su))
                        need("dve", v)
                        return V(dve.tensor_scalar(prob[:, j, :], prob[:, j, :], rc, None, ALU.mult))

                    def turn(j, b, v, dst, dst0, *waits):
                        need("pe", v, bank_free[b])
                        for t, (c0, n) in enumerate(TILES):
                            m = pe.transpose(bank[b][0:n, t * P:(t + 1) * P], prob[:, j, c0:c0 + n], ident)
                        m = M(m)
                        prob_free[j] = m
                        need("act", m, *waits)
                        a = A(act.activation(dst0, bank[b][0:META, 0:P], ACT.Copy))
                        a2 = A(act.activation(dst, bank[b][:, P:3 * P].rearrange("p (t n) -> p t n", t=2), ACT.Copy))
                        evacuated(b, a2)
                        return a2

                    bS, bT, bO = ATB[0], ATB[1], ATB[2]
                    need("pe", ev["rope"], bank_free[bS])
                    for g in range(2):
                        for par in range(2):
                            r0 = 64 * g + 32 * par
                            hr = slice(64 * par, 64 * par + 64)
                            m = pe.matmul(bank[bS][r0:r0 + 32, 0:T], qb_meta[hr, 2 * g:2 * g + 2, :].rearrange("p a t -> p (a t)"),
                                          kdup[hr, g, :], start=True, stop=True)
                    m = M(m)
                    need("dve", m)
                    v = softmax(bS, 0)
                    yield
                    e_lt = turn(0, bT, v, lt[:, 1:3, :], lt[0:META, 0, :])
                    pt_free = [None, None]
                    for p in range(4):
                        for par in range(2):
                            h = 2 * p + par
                            g = h // 4
                            hr = slice(64 * par, 64 * par + 64)
                            probs = []
                            for t in (1, 2):
                                c0, n = TILES[t]
                                b = (bS, bT)[t - 1]
                                need("pe", bank_free[b])
                                m = M(pe.matmul(bank[b][:, 0:T], qb[hr, p, c0:c0 + n], kdup[hr, g, :], start=True, stop=True))
                                need("dve", m)
                                probs.append(softmax(b, t - 1))
                            yield
                            for t in (1, 2):
                                b = (bS, bT)[t - 1]
                                e_pt = turn(t - 1, b, probs[t - 1], pt[:, par, 1:3, (t - 1) * P:t * P],
                                            pt[0:META, par, 0, (t - 1) * P:t * P], pt_free[par])
                            yield
                            need("pe", e_pt, e_lt, ev["vb"], bank_free[bO] if par == 0 else None)
                            o = bank[bO][64 * par:64 * par + 64, :]
                            lc = 64 * g + 32 * par + 16 * (p % 2)
                            for t, (c0, n) in enumerate(TILES):
                                pe.matmul(o[:, META:T], vb[0:n, t, g * 64:g * 64 + 64], pt[0:n, par, t, :], start=t == 0, stop=t == 2)
                            for t, (c0, n) in enumerate(TILES):
                                m = pe.matmul(o[:, 0:META], vb[0:n, t, g * 64:g * 64 + 64], lt[0:n, t, lc:lc + META],
                                              start=t == 0, stop=t == 2)
                            m = M(m)
                            pt_free[par] = m
                        need("act", m)
                        b_ready[p] = split_rows(b_hi[:, p, :], b_lo[:, p, :], bank[bO][:, 0:T], m)
                        evacuated(bO, *b_ready[p])

                ATB = [5, 6, 7]

                h_use = [None]

                def r_out(j, b):
                    def post(m):
                        need("act", m)
                        e = A(act.activation(r_act[:, j, :], bank[b][:, 0:T], ACT.Copy))
                        evacuated(b, e)
                        ev["r", j] = e
                        if j == 3:
                            need("act", e)
                            ev["silu_r"] = A(act.activation(r_act[:, :, :], r_act[:, :, :], ACT.Silu))
                    return post

                def half_tiles(bs, xh, xl, ready):
                    def work(wh, wl):
                        for j, b in enumerate(bs):
                            need("pe", bank_free[b])
                            for k in range(4):
                                need("pe", ready[k])
                                s = slice((4 * j + k) * P, (4 * j + k + 1) * P)
                                m = product(bank[b][:, 0:T], wh[:, s], wl[:, s], xh[:, k, :], xl[:, k, :], k == 0, k == 3)
                        return m
                    return work

                def merged_a(ms, bs):
                    def post(m):
                        for mt, b in zip(ms, bs):
                            need("dve", m, ev["sig"])
                            v = V(dve.tensor_tensor(gates[:, mt, :], gates[:, mt, :], bank[b][:, 0:T], ALU.mult))
                            evacuated(b, v)
                            ev["ya", mt] = v
                    return post

                def merged_b(ms, bs):
                    def post(m):
                        for mt, b in zip(ms, bs):
                            need("dve", m, ev["ya", mt])
                            v = V(dve.tensor_tensor(gates[:, 8 + mt, :], gates[:, 8 + mt, :], bank[b][:, 0:T], ALU.mult))
                            evacuated(b, v)
                            need("dve", v)
                            v = V(dve.tensor_tensor(gates[:, mt, :], gates[:, mt, :], gates[:, 8 + mt, :], ALU.add))
                            y_ready[mt] = split_rows(y_hi[:, mt, :], y_lo[:, mt, :], gates[:, mt, :], v, xn_free[0])
                    return post

                def mixed_out(mt, b):
                    def post(m):
                        need("dve", m)
                        v = V(dve.tensor_tensor(x[:, mt, :], x[:, mt, :], bank[b][:, 0:T], ALU.add))
                        evacuated(b, v)
                        sum_squares_of(x[:, mt, :], v)
                    return post

                def last_gate(m):
                    gate_out(15, 1)(m)
                    xn_free[0] = m
                    need("act", ev["g", 15])
                    ev["sig"] = A(act.activation(gates[:, :, :], gates[:, :, :], ACT.Sigmoid))

                def pair(c, works, posts):
                    n = len(works)
                    return Pair([mix_src(c), mix_src(c + 1) if n == 4 else None], [1024] * n + [0] * (4 - n),
                                works + [None] * (4 - n), posts + [None] * (4 - n))

                def ytile(b):
                    return feature_tile(b, P, T, KD, y_hi, y_lo, y_ready)

                ab, cd = [0, 1], [2, 3]
                pairs = [
                    pair(0, [xtile(0), xtile(1), xtile(2), xtile(3)],
                         [copy_to(qa[:, 0, :], 0, ("qa", 0), GLA_DK ** -0.5), copy_to(qa[:, 1, :], 1, ("qa", 1), GLA_DK ** -0.5),
                          copy_to(ka[:, 0, :], 2, ("ka", 0)), copy_to(ka[:, 1, :], 3, ("ka", 1))]),
                    pair(2, [token_tiles([4, 5, 6], [P * j] * 3) for j in range(4)], [None, None, None, v_out]),
                    pair(4, [xtile(j % 2) for j in range(4)], [copy_to(qb[:, j, :], j % 2, ("qb", j)) for j in range(4)]),
                    pair(6, [xtile(0), token_tiles([1, 1, 1], [0, P, 2 * P]), xtile(0), xtile(1)],
                         [copy_to(kb[:, :], 0, "kb"), vb_out, r_out(0, 0), r_out(1, 1)]),
                    pair(8, [xtile(j % 2) for j in range(4)],
                         [r_out(2, 0), r_out(3, 1), gate_out(0, 0), gate_out(1, 1)]),
                ]
                for i in range(3):
                    pairs.append(pair(10 + 2 * i, [xtile(j % 2) for j in range(4)],
                                      [gate_out(2 + 4 * i + j, j % 2) for j in range(4)]))

                def of_a(bs):
                    return half_tiles(bs, a_hi, a_lo, a_ready)

                def of_b(bs):
                    return half_tiles(bs, b_hi, b_lo, b_ready)
                pairs.append(pair(16, [xtile(0), xtile(1), of_a(ab), of_a(cd)],
                                  [gate_out(14, 0), last_gate, merged_a([0, 1], ab), merged_a([2, 3], cd)]))
                pairs.append(pair(18, [of_a(ab), of_a(cd), of_b(ab), of_b(cd)],
                                  [merged_a([4, 5], ab), merged_a([6, 7], cd), merged_b([0, 1], ab), merged_b([2, 3], cd)]))
                pairs.append(pair(20, [of_b(ab), of_b(cd), ytile(0), ytile(1)],
                                  [merged_b([4, 5], ab), merged_b([6, 7], cd), mixed_out(0, 0), mixed_out(1, 1)]))
                pairs.append(pair(22, [ytile(2), ytile(3), ytile(0), ytile(1)], [mixed_out(2 + j, (2 + j) % 4) for j in range(4)]))
                pairs.append(pair(24, [ytile(2), ytile(3)], [mixed_out(6, 2), mixed_out(7, 3)]))

                def everything(engines):
                    for e in engines:
                        need(e, *[Event(line, ct.count[line]) for line in ("pe", "act", "dve", "ada")])

                def reduce_ada(f):
                    need("pe", ada["used"], bank_free[0])
                    for j in range(48):
                        m = pe.matmul(bank[0][:, j:j + 1], acc[:, j * P:(j + 1) * P], ones[:, 0:1], start=True, stop=True)
                    m = M(m)
                    need("dve", m)
                    mod = mod_all[:, bass.ds(l, 1), :]
                    v = V(dve.tensor_tensor(mod, bank[0][:, 0:48].rearrange("p (a n) -> p a n", a=1),
                                            bada[:, :].rearrange("p (a n) -> p a n", a=1) if f == 0 else mod, ALU.add))
                    evacuated(0, v)

                start(gate_up(0, 0))
                need("act", small)
                need("dve", small)
                clear_sumsq()
                for k in range(KD):
                    sum_squares_of(x[:, k, :], None)
                ffn(0, v1[:, V_GAIN:V_GAIN + 8], pairs[0])
                reduce_ada(0)
                normalise(TA, v1[:, V_GAIN + 8:V_GAIN + 16])
                clear_sumsq()
                everything(["act", "dve"])
                log_gates()
                for i, p in enumerate(pairs):
                    if i == 2:
                        linear = [gla()]
                    if i == 3:
                        softm = [attention()]
                    if i == 8:
                        finish(linear)
                    side = (linear if 2 <= i < 8 else []) + (softm if 3 <= i < 9 else [])
                    if i == 9:
                        side = softm
                    run_pair(p, pairs[i + 1] if i + 1 < len(pairs) else gate_up(1, 0), side,
                             stop_side=2 if i == 9 else None)
                xn_free[0] = S.unit_free[1]
                everything(["act", "dve", "pool"])
                ffn(1, v1[:, V_GAIN + 16:V_GAIN + 24], None)
                reduce_ada(1)

            ct.kept = {"ada": 16 * 24}
            with nc.Fori(0, L) as l:
                ct.layer = l
                layer1(l)
                assert ct.count["ada"] == ct.kept["ada"]
                ct.new_layer()
        N = SEQ
        TB = slice(META, T)
        TN = slice(0, N)

        def reset_layer():
            for i in range(8):
                bank_free[i] = None
            S.landed, S.split_of, S.unit_free, S.raw_users = [None] * 2, [None] * 4, [None] * 4, [[], []]
            sq_free[0] = sq_free[1] = sumsq_free[0] = xn_free[0] = None
            full_free[0], full_free[1] = [], []

        def clear_sumsq():
            need("dve", sumsq_free[0])
            sumsq_free[0] = V(dve.memset(sumsq[:, :], 0.0))

        def add_squares(xk, ev):
            n = xk.shape[-1]
            need("dve", ev, sq_free[0])
            v = V(dve.tensor_tensor(sq[:, 0:n], xk, xk, ALU.mult))
            need("dve", v, sumsq_free[0])
            v = V(dve.tensor_tensor(sumsq[:, TB], sumsq[:, TB], sq[:, 0:n], ALU.add))
            sq_free[0] = sumsq_free[0] = v

        reset_layer()
        clear_sumsq()
        for k in range(KD):
            add_squares(x[:, k, TB], None)
        normed = []
        normalise(TB, vg[:, G_FN:G_FN + 8], into=normed)

        place[0] = block_start
        v2 = sb("v2", [P, V2_ALL])
        mod = sb("mod", [P, 48])
        gain = sb("gain", [P, 2, KD])
        cos2 = sb("cos2", [96, N])
        sin2 = sb("sin2", [96, N])
        angle = sb("angle", [96, N])
        turns = sb("turns", [96, N])
        rest = sb("rest", [96, N])
        posi = sb("posi", [96, N], I32)
        shared_start = place[0]
        f_hi = sb("f_hi", [P, KF2, N], F32R)
        f_lo = sb("f_lo", [P, KF2, N], F32R)
        place[0] = shared_start
        gates2 = sb("gates2", [P, 16, N])
        u_pool = sb("u_pool", [P, 4, T])
        s_pool = sb("s_pool", [P, 2, T])
        p_full = sb("p_full", [P, 4, N])
        p_hi = sb("p_hi", [P, 4, N], F32R)
        p_lo = sb("p_lo", [P, 4, N], F32R)
        cq = sb("cq", [P, 3, N])
        ckv = sb("ckv", [P, 2, N])
        cq_hi = sb("cq_hi", [P, 3, N], F32R)
        cq_lo = sb("cq_lo", [P, 3, N], F32R)
        ckv_hi = sb("ckv_hi", [P, 2, N], F32R)
        ckv_lo = sb("ckv_lo", [P, 2, N], F32R)
        k_rot = sb("k_rot", [96, N])
        q_all = sb("q_all", [96, MH, N])
        k_all = sb("k_all", [96, MH, N])
        v_tok = sb("v_tok", [P, 2, 512])
        r_tmp = sb("r_tmp", [96, 2, N])
        scores = sb("scores", [P, 2, 3 * P])
        pt2 = sb("pt2", [P, 2, 3 * P])
        stat2 = sb("stat2", [P, 32])
        a2_hi = sb("a2_hi", [P, 4, N], F32R)
        a2_lo = sb("a2_lo", [P, 4, N], F32R)
        pw_hi, pw_lo = p_hi, p_lo
        RP = slice(64, 96)

        def rope_tables():
            two_pi = 2 * np.pi
            c1 = 6.28125
            c2 = float(np.float32(np.floor((two_pi - c1) * 2 ** 20) / 2 ** 20))
            c3 = float(np.float32(two_pi - c1 - c2))
            magic = float(1.5 * 2 ** 23)
            p = done("small", sp.dma_start(posi[RP, :], pos), 16)
            need("dve", p)

            def step(ins):
                need("dve", V(ins))
            step(dve.tensor_copy(rest[RP, :], posi[RP, :]))
            step(dve.tensor_scalar(angle[RP, :], rest[RP, :], cst[RP, C_INV:C_INV + 1], None, ALU.mult))
            step(dve.tensor_scalar(turns[RP, :], angle[RP, :], 1.0 / two_pi, magic, ALU.mult, ALU.add))
            step(dve.tensor_scalar(turns[RP, :], turns[RP, :], -magic, None, ALU.add))
            for c in (c1, c2, c3):
                step(dve.scalar_tensor_tensor(out=angle[RP, :], in0=turns[RP, :], scalar=-c, in1=angle[RP, :],
                                              op0=ALU.mult, op1=ALU.add))
            step(dve.tensor_scalar(rest[RP, :], angle[RP, :], np.pi / 2, None, ALU.add))
            step(dve.tensor_scalar(turns[RP, :], rest[RP, :], np.pi, None, ALU.is_gt))
            step(dve.scalar_tensor_tensor(out=rest[RP, :], in0=turns[RP, :], scalar=-two_pi, in1=rest[RP, :],
                                          op0=ALU.mult, op1=ALU.add))
            top = float(np.nextafter(np.float32(np.pi), np.float32(0)))
            for buf in (angle, rest):
                step(dve.tensor_scalar(buf[RP, :], buf[RP, :], top, -top, ALU.min, ALU.max))
            need("act", Event("dve", ct.count["dve"]))
            A(act.activation(sin2[RP, :], angle[RP, :], ACT.Sin))
            A(act.activation(cos2[RP, :], rest[RP, :], ACT.Sin))

        rope_tables()
        ct.kept = {}
        ct.sem.pop("ada")
        ct.new_layer()

        def layer2(l):
            reset_layer()
            small = done("vec", act.dma_start(v2[:, :], vec2[l]), 16)

            def w2_src(off, w, step=0, i=0):
                return w2[l, :, bass.ds(off + i * step, w)]

            def block_pair(c, works, posts, widths):
                n = len(works)
                return Pair([w2_src(M2_OFF[c], M2_WIDTH[c]), w2_src(M2_OFF[c + 1], M2_WIDTH[c + 1]) if widths[2] else None],
                            widths, works + [None] * (4 - n), posts + [None] * (4 - n))

            ev = {}
            cq_ready, ckv_ready, p_ready, pw_ready, a2_ready, y_ready = [None] * 3, [None] * 2, [None] * 4, [None] * 4, [None] * 4, [None] * KD

            def xtile(b, rows=P, ps_rows=None, step=P):
                return feature_tile(b, rows, N, KD, xn_hi, xn_lo, xn_ready, ps_rows=ps_rows, step=step)

            def keep(dst, b, key, rows=slice(0, P), then=None):
                def post(m):
                    need("act", m)
                    ev[key] = A(act.activation(dst, bank[b][rows, 0:N], ACT.Copy))
                    evacuated(b, ev[key])
                    if then is not None:
                        then()
                return post

            def low_rank_norm(src, n_k, width, g0, hi, lo, ready, keys, b=7):
                need("dve", [ev[k] for k in keys], sq_free[1])
                for k in range(n_k):
                    dst = sq2 if k == 0 else gate[:, 0, :]
                    need("dve", gate_free2[0] if k else None)
                    v = V(dve.tensor_tensor(dst[:, 0:N], src[:, k, :], src[:, k, :], ALU.mult))
                    if k:
                        need("dve", v)
                        v = V(dve.tensor_tensor(sq2[:, 0:N], sq2[:, 0:N], gate[:, 0, 0:N], ALU.add))
                        need("dve", v)
                need("pe", v, bank_free[b])
                m = M(pe.matmul(bank[b][:, 0:N], ones, sq2[:, 0:N], start=True, stop=True))
                sq_free[1] = m
                r = inverse_root(gate[:, 1, 0:N], bank[b][:, 0:N], 1.0 / width, m, gate_free2[0])
                evacuated(b, r)
                need("dve", r)
                for k in range(n_k):
                    v = V(dve.scalar_tensor_tensor(out=src[:, k, :], in0=src[:, k, :], scalar=v2[:, g0 + k:g0 + k + 1],
                                                   in1=gate[:, 1, 0:N], op0=ALU.mult, op1=ALU.mult))
                    gate_free2[0] = v
                    ready[k] = split_rows(hi[:, k, :], lo[:, k, :], src[:, k, :], v)

            gate_free2 = [None]

            def k_rope():
                need("pe", ev["krope"], bank_free[6], bank_free[7])
                pe.matmul(bank[6][RP, 0:N], cst[0:32, C_ID:C_ID + 32], k_rot[0:32, :], start=True, stop=True)
                m = M(pe.matmul(bank[7][RP, 0:N], cst[0:32, C_R32:C_R32 + 32], k_rot[0:32, :], start=True, stop=True))
                need("dve", m, r_free[0])
                v = V(dve.tensor_tensor(r_tmp[RP, 0, :], bank[7][RP, 0:N], sin2[RP, :], ALU.mult))
                evacuated(7, v)
                w = V(dve.tensor_tensor(k_rot[RP, :], bank[6][RP, 0:N], cos2[RP, :], ALU.mult))
                evacuated(6, w)
                need("dve", w)
                v = V(dve.tensor_tensor(k_rot[RP, :], k_rot[RP, :], r_tmp[RP, 0, :], ALU.add))
                r_free[0] = v
                need("act", v)
                for h in range(MH):
                    e = A(act.activation(k_all[RP, h, :], k_rot[RP, :], ACT.Copy))
                ev["kr"] = e

            r_free = [None]

            def pooling():
                for g, w in enumerate(POOL_W):
                    need("pool", ev["pool", g])
                    cur = u_pool[:, g, :]
                    s, i = 1, 0
                    while s < w:
                        dst = s_pool[:, i, :]
                        p = G(pool.tensor_tensor(dst[:, META:T], cur[:, META:T], cur[:, META - s:T - s], ALU.add))
                        need("pool", p)
                        cur, s, i = dst, 2 * s, 1 - i
                    need("pool", ev.get("p_used"))
                    G(pool.tensor_tensor(p_full[:, g, 0:16], cur[:, META:META + 16], cst[:, C_CNT + 16 * g:C_CNT + 16 * g + 16], ALU.mult))
                    p = G(pool.tensor_scalar(p_full[:, g, 16:N], cur[:, META + 16:T], 1.0 / w, None, ALU.mult))
                    need("pool", p)
                    p = G(pool.tensor_tensor(p_full[:, g, :], p_full[:, g, :], u_pool[:, g, META:T], ALU.subtract))
                    need("pool", p)
                    ev["p", g] = p

            def pooled_split():
                for g in range(4):
                    p_ready[g] = split_rows(p_hi[:, g, :], p_lo[:, g, :], p_full[:, g, :], ev["p", g])

            def queries(h0, bs):
                def work(wh, wl):
                    for j in range(4):
                        b = bs[j]
                        need("pe", bank_free[b])
                        for k in range(3):
                            need("pe", cq_ready[k])
                            s = slice((3 * j + k) * QK, (3 * j + k + 1) * QK)
                            m = product(bank[b][0:QK, 0:N], wh[:, s], wl[:, s], cq_hi[:, k, :], cq_lo[:, k, :], k == 0, k == 2)
                    return m
                return work

            def queries_out(h0, bs):
                def post(m):
                    need("act", m)
                    for j in range(4):
                        e = A(act.activation(q_all[:, h0 + j, :], bank[bs[j]][0:QK, 0:N], ACT.Copy))
                        evacuated(bs[j], e)
                    ev["q", h0] = e
                return post

            def q_rope(h0):
                for j in range(0, 4, 2):
                    h = h0 + j
                    need("pe", ev["q", h0], bank_free[7])
                    m = M(pe.matmul(bank[7][RP, 0:2 * N], cst[RP, C_R32:C_R32 + 32],
                                    q_all[RP, h:h + 2, :].rearrange("p h n -> p (h n)"), start=True, stop=True))
                    need("dve", m, r_free[0])
                    for i in range(2):
                        v = V(dve.tensor_tensor(r_tmp[RP, i, :], bank[7][RP, i * N:(i + 1) * N], sin2[RP, :], ALU.mult))
                        w = V(dve.tensor_tensor(q_all[RP, h + i, :], q_all[RP, h + i, :], cos2[RP, :], ALU.mult))
                    evacuated(7, v)
                    need("dve", w)
                    v = V(dve.tensor_tensor(q_all[RP, h:h + 2, :], q_all[RP, h:h + 2, :], r_tmp[RP, :, :], ALU.add))
                    r_free[0] = v
                ev["qr", h0] = v

            def keys(wh, wl):
                for h in range(MH):
                    b = h // 2
                    need("pe", bank_free[b])
                    for k in range(2):
                        need("pe", ckv_ready[k])
                        s = slice((2 * h + k) * 64, (2 * h + k + 1) * 64)
                        m = product(bank[b][0:64, N * (h % 2):N * (h % 2) + N], wh[:, s], wl[:, s], ckv_hi[:, k, :], ckv_lo[:, k, :],
                                    k == 0, k == 1)
                return m

            def keys_out(m):
                need("act", m)
                for b in range(4):
                    e = A(act.activation(k_all[0:64, 2 * b:2 * b + 2, :].rearrange("p h n -> p (h n)"), bank[b][0:64, :], ACT.Copy))
                    evacuated(b, e)
                ev["k"] = e

            def values(wh, wl):
                for t in range(2):
                    need("pe", bank_free[t])
                    cs = slice(t * P, (t + 1) * P)
                    for k in range(2):
                        s = slice(k * 512, (k + 1) * 512)
                        pe.matmul(bank[t][:, :], ckv_hi[:, k, cs], wh[:, s], start=k == 0, stop=False)
                        pe.matmul(bank[t][:, :], ckv_lo[:, k, cs], wh[:, s], start=False, stop=False)
                        m = pe.matmul(bank[t][:, :], ckv_hi[:, k, cs], wl[:, s], start=False, stop=k == 1)
                return m

            def values_out(m):
                need("act", m)
                for t in range(2):
                    e = A(act.activation(v_tok[:, t, :], bank[t][:, :], ACT.Copy))
                    evacuated(t, e)
                ev["v"] = e

            def attention2():
                scale = QK ** -0.5
                p_free, t_free = [None, None], [None, None]
                for h in range(MH):
                    j = h % 2
                    bS, bT, bO = 4 + j, 6, 7
                    need("pe", ev["kr"], ev["k"], ev["qr", 4 * (h // 4)], bank_free[bS])
                    pe.matmul(bank[bS][:, 0:P], q_all[:, h, 0:P], k_all[:, h, 0:P], start=True, stop=True)
                    m = M(pe.matmul(bank[bS][:, P:3 * P], q_all[:, h, P:2 * P], k_all[:, h, :], start=True, stop=True))
                    yield
                    need("dve", m, p_free[j])
                    c = 8 * (h % 4)
                    for t, cs in enumerate((slice(0, P), slice(P, 3 * P))):
                        v = V(dve.tensor_tensor(scores[:, j, cs], bank[bS][:, cs], cst[:, C_MASK + cs.start:C_MASK + cs.stop], ALU.add))
                        need("dve", v)
                        v = V(dve.reduce_max(stat2[:, c + t:c + t + 1], scores[:, j, cs], AX))
                    evacuated(bS, v)
                    need("dve", v)
                    v = V(dve.tensor_scalar(stat2[:, c + 2:c + 4], stat2[:, c:c + 2], -scale, None, ALU.mult))
                    need("act", v)
                    for t, cs in enumerate((slice(0, P), slice(P, 3 * P))):
                        a = A(act.activation(scores[:, j, cs], scores[:, j, cs], ACT.Exp, bias=stat2[:, c + 2 + t:c + 3 + t],
                                             scale=scale, accum_out=stat2[:, c + 4 + t:c + 5 + t]))
                    need("dve", a)
                    v = V(dve.reciprocal(stat2[:, c + 6:c + 8], stat2[:, c + 4:c + 6]))
                    need("dve", v)
                    for t, cs in enumerate((slice(0, P), slice(P, 3 * P))):
                        v = V(dve.tensor_scalar(scores[:, j, cs], scores[:, j, cs], stat2[:, c + 6 + t:c + 7 + t], None, ALU.mult))
                    yield
                    need("pe", v, bank_free[bT])
                    for t in range(3):
                        m = pe.transpose(bank[bT][:, t * P:(t + 1) * P], scores[:, j, t * P:(t + 1) * P], ident)
                    m = M(m)
                    p_free[j] = m
                    need("act", m, t_free[j])
                    a = A(act.activation(pt2[:, j, :], bank[bT][:, 0:3 * P], ACT.Copy))
                    evacuated(bT, a)
                    need("pe", a, ev["v"], bank_free[bO] if j == 0 else None)
                    o = bank[bO][64 * j:64 * j + 64, :]
                    pe.matmul(o[:, 0:N], v_tok[:, 0, 64 * h:64 * h + 64], pt2[:, j, 0:2 * P], start=True, stop=False)
                    m = M(pe.matmul(o[:, P:N], v_tok[:, 1, 64 * h:64 * h + 64], pt2[:, j, 2 * P:3 * P], start=False, stop=True))
                    t_free[j] = m
                    if j:
                        a2_ready[h // 2] = split_rows(a2_hi[:, h // 2, :], a2_lo[:, h // 2, :], bank[bO][:, 0:N], m)
                        evacuated(bO, *a2_ready[h // 2])

            def gate2_out(j, b, then=None):
                return keep(gates2[:, j, :], b, ("g", j), then=then)

            def pool_out(g, b):
                def post(m):
                    need("act", m)
                    ev["pool", g] = A(act.activation(u_pool[:, g, META:T], bank[b][:, 0:N], ACT.Copy))
                    evacuated(b, ev["pool", g])
                return post

            def pool_project(wh, wl):
                for g in range(4):
                    b = g % 2
                    o = bank[b][:, N * (g // 2):N * (g // 2) + N]
                    need("pe", bank_free[b], p_ready[g])
                    s = slice(g * P, (g + 1) * P)
                    m = product(o, wh[:, s], wl[:, s], p_hi[:, g, :], p_lo[:, g, :], True, True)
                return m

            def pool_projected(m):
                need("act", m)
                for g in range(4):
                    o = bank[g % 2][:, N * (g // 2):N * (g // 2) + N]
                    a = A(act.activation(p_full[:, g, :], o, ACT.Copy, scale=v2[:, V_PS + g:V_PS + g + 1]))
                    evacuated(g % 2, a)
                    pw_ready[g] = split_rows(pw_hi[:, g, :], pw_lo[:, g, :], p_full[:, g, :], a)

            def half_tiles(bs, xh, xl, ready):
                def work(wh, wl):
                    for j, b in enumerate(bs):
                        need("pe", bank_free[b])
                        for k in range(4):
                            need("pe", ready[k])
                            s = slice((4 * j + k) * P, (4 * j + k + 1) * P)
                            m = product(bank[b][:, 0:N], wh[:, s], wl[:, s], xh[:, k, :], xl[:, k, :], k == 0, k == 3)
                    return m
                return work

            def merged_a(ms, bs):
                def post(m):
                    for mt, b in zip(ms, bs):
                        need("dve", m, ev["sig"])
                        v = V(dve.tensor_tensor(gates2[:, mt, :], gates2[:, mt, :], bank[b][:, 0:N], ALU.mult))
                        evacuated(b, v)
                        ev["ya", mt] = v
                return post

            def merged_b(ms, bs):
                def post(m):
                    for mt, b in zip(ms, bs):
                        need("dve", m, ev["ya", mt])
                        v = V(dve.tensor_tensor(gates2[:, 8 + mt, :], gates2[:, 8 + mt, :], bank[b][:, 0:N], ALU.mult))
                        evacuated(b, v)
                        need("dve", v)
                        v = V(dve.tensor_tensor(gates2[:, mt, :], gates2[:, mt, :], gates2[:, 8 + mt, :], ALU.add))
                        y_ready[mt] = split_rows(xn_hi[:, mt, TN], xn_lo[:, mt, TN], gates2[:, mt, :], v, xn_free[0])
                return post

            def residual(mt, b, g):
                def post(m):
                    need("dve", m)
                    v = V(dve.scalar_tensor_tensor(out=x[:, mt, TB], in0=bank[b][:, 0:N], scalar=mod[:, g + mt:g + mt + 1],
                                                   in1=x[:, mt, TB], op0=ALU.mult, op1=ALU.add))
                    evacuated(b, v)
                    add_squares(x[:, mt, TB], v)
                return post

            def gates_done():
                xn_free[0] = S.unit_free[1]
                need("act", ev["g", 15])
                ev["sig"] = A(act.activation(gates2[:, :, :], gates2[:, :, :], ACT.Sigmoid))

            ab, cd = [0, 1], [2, 3]
            K4 = [1024] * 4

            def of_p(bs):
                return half_tiles(bs, pw_hi, pw_lo, pw_ready)

            def of_a(bs):
                return half_tiles(bs, a2_hi, a2_lo, a2_ready)

            def ytile(b):
                return feature_tile(b, P, N, KD, xn_hi, xn_lo, y_ready)

            pairs = [
                block_pair(0, [xtile(j) for j in range(4)],
                           [keep(cq[:, 0, :], 0, "cq0"), keep(cq[:, 1, :], 1, "cq1"),
                            keep(cq[:, 2, :], 2, "cq2", then=lambda: low_rank_norm(cq, 3, QL, V_QG, cq_hi, cq_lo, cq_ready, ["cq0", "cq1", "cq2"])),
                            keep(ckv[:, 0, :], 3, "kv0")], K4),
                block_pair(2, [xtile(0), xtile(1, 32, step=32), xtile(2), xtile(3)],
                           [keep(ckv[:, 1, :], 0, "kv1", then=lambda: low_rank_norm(ckv, 2, KVL, V_KVG, ckv_hi, ckv_lo, ckv_ready, ["kv0", "kv1"])),
                            keep(k_rot[0:32, :], 1, "krope", rows=slice(0, 32), then=k_rope),
                            pool_out(0, 2), pool_out(1, 3)], [1024, 256, 1024, 1024]),
                block_pair(4, [xtile(0), xtile(1), queries(0, [2, 3, 4, 5]), queries(4, [0, 1, 2, 3])],
                           [pool_out(2, 0), pool_out(3, 1), queries_out(0, [2, 3, 4, 5]), queries_out(4, [0, 1, 2, 3])],
                           [1024, 1024, 1152, 1152]),
                block_pair(6, [keys, values, xtile(2), xtile(3)],
                           [keys_out, values_out, gate2_out(0, 2), gate2_out(1, 3)], K4),
            ]
            for i in range(3):
                pairs.append(block_pair(8 + 2 * i, [xtile(j) for j in range(4)], [gate2_out(2 + 4 * i + j, j) for j in range(4)], K4))
            pairs.append(block_pair(14, [xtile(0), xtile(1), pool_project],
                                    [gate2_out(14, 0), gate2_out(15, 1, then=gates_done), pool_projected], [1024, 1024, 512, 0]))
            pairs.append(block_pair(16, [of_p(ab), of_p(cd), of_a(ab), of_a(cd)],
                                    [merged_a([0, 1], ab), merged_a([2, 3], cd), merged_b([0, 1], ab), merged_b([2, 3], cd)], K4))
            pairs.append(block_pair(18, [of_p(ab), of_p(cd), of_a(ab), of_a(cd)],
                                    [merged_a([4, 5], ab), merged_a([6, 7], cd), merged_b([4, 5], ab), merged_b([6, 7], cd)], K4))
            for i in range(2):
                pairs.append(block_pair(20 + 2 * i, [ytile(j) for j in range(4)], [residual(4 * i + j, j, 16) for j in range(4)], K4))

            f_last = [None]

            def ff1(i):
                def squared(j):
                    def post(m):
                        q = j % 2
                        need("dve", m, full_free[q])
                        v = V(dve.tensor_scalar(full[:, q, 0:N], bank[j][:, 0:N], 0.0, None, ALU.max))
                        evacuated(j, v)
                        need("dve", v)
                        v = V(dve.tensor_tensor(full[:, q, 0:N], full[:, q, 0:N], full[:, q, 0:N], ALU.mult))
                        hh, hl = f_hi[:, bass.ds(4 * i + j, 1), :], f_lo[:, bass.ds(4 * i + j, 1), :]
                        fj = full[:, q:q + 1, 0:N]
                        need("act", v)
                        a = A(act.activation(hh, fj, ACT.Copy))
                        need("dve", a)
                        v = V(dve.tensor_tensor(hl, fj, hh.bitcast(F32), ALU.subtract))
                        full_free[q] = [a, v]
                        f_last[0] = [a, v]
                    return post
                return Pair([w2_src(W2_FF1, 2048, 4096, i), w2_src(W2_FF1 + 2048, 2048, 4096, i)], K4,
                            [xtile(j) for j in range(4)], [squared(j) for j in range(4)])

            def ff2(g, half):
                def part(c, j):
                    def work(wh, wl):
                        b = 4 + j
                        if half == 0 and c == 0:
                            need("pe", bank_free[b])
                        need("pe", f_last[0])
                        for k in range(8):
                            kk = 16 * half + 8 * c + k
                            s = slice(k * P, (k + 1) * P)
                            m = product(bank[b][:, 0:N], wh[:, s], wl[:, s], f_hi[:, kk, :], f_lo[:, kk, :], kk == 0, kk == KF2 - 1)
                        return m
                    return work

                def add(j):
                    def post(m):
                        xk = x[:, bass.ds(2 * g + j, 1), TB]
                        need("dve", m)
                        o = bank[4 + j][:, 0:N].rearrange("p (a t) -> p a t", a=1)
                        v = V(dve.tensor_scalar(full[:, 0:1, 0:N], o, mod[:, bass.ds(40 + 2 * g + j, 1)], None, ALU.mult))
                        evacuated(4 + j, v)
                        need("dve", v)
                        v = V(dve.tensor_tensor(xk, xk, full[:, 0:1, 0:N], ALU.add))
                        add_squares(xk.rearrange("p a t -> p (a t)"), v)
                    return post
                o = W2_FF2 + half * 4096
                return Pair([w2_src(o, 2048, 8192, g), w2_src(o + 2048, 2048, 8192, g)], K4,
                            [part(0, 0), part(0, 1), part(1, 0), part(1, 1)], [None, None] + ([add(0), add(1)] if half else [None, None]))

            start(pairs[0])
            for b in (u_pool, s_pool):
                z = G(pool.memset(b[:, :, 0:META], 0.0))
            need("pool", z)
            v = V(dve.tensor_copy(mod[:, :].rearrange("p (a n) -> p a n", a=1), mod_all[:, bass.ds(l, 1), :]))
            need("dve", v, small)
            need("act", v, small)
            for i, (g, sc) in enumerate(((V_LN1, 8), (V_LN2, 32))):
                v = V(dve.scalar_tensor_tensor(out=gain[:, i, :], in0=mod[:, sc:sc + 8], scalar=1.0, in1=v2[:, g:g + 8],
                                               op0=ALU.add, op1=ALU.mult))
            need("dve", v)
            clear_sumsq()
            for k in range(KD):
                add_squares(x[:, k, TB], None)
            normalise(TB, gain[:, 0, :], mod[:, 0:8])
            clear_sumsq()
            side = []
            for i, p in enumerate(pairs):
                if i == 3:
                    q_rope(0)
                    q_rope(4)
                    pooling()
                if i == 4:
                    side = [attention2()]
                if i == 7:
                    pooled_split()
                if i == 8:
                    finish(side)
                    side = []
                run_pair(p, pairs[i + 1] if i + 1 < len(pairs) else ff1(0), side)
            xn_free[0] = S.unit_free[3]
            for e in ("act", "dve"):
                need(e, *[Event(line, ct.count[line]) for line in ("pe", "act", "dve", "pool")])
            normalise(TB, gain[:, 1, :], mod[:, 24:32])
            clear_sumsq()
            ct.repeat(8, lambda i: run_pair(ff1(i), ff2(0, 0) if isinstance(i, int) and i == 7 else ff1(i + 1)))

            def last_step(g):
                run_pair(ff2(g, 0), ff2(g, 1))
                run_pair(ff2(g, 1), None if isinstance(g, int) and g == 3 else ff2(g + 1, 0))
            ct.repeat(4, last_step)

        with nc.Fori(0, L) as l2:
            ct.layer = l2
            layer2(l2)
            ct.new_layer()

        reset_layer()
        clear_sumsq()
        for k in range(KD):
            add_squares(x[:, k, TB], None)
        normed = []
        normalise(TB, vg[:, G_FG:G_FG + 8], into=normed)
        need("sp", normed)
        sp.dma_start(out, x[:, :, TB]).then_inc(ct.out_sem, 16)
        sp.wait_ge(ct.out_sem, 16)


def _units(w, cols):
    k = w.shape[0] // P
    w = w.reshape(k, P, w.shape[1] // cols, cols)
    return w.transpose(1, 2, 0, 3).reshape(P, -1)


def _columns(v):
    return v.reshape(-1, P).T


def _layer1_weights(i, l):
    parts = []
    for f in range(2):
        g, u = _units(i["ffn_w_gate"][l, f], P), _units(i["ffn_w_up"][l, f], P)
        gu = np.stack([g.reshape(P, FG, 2048), u.reshape(P, FG, 2048)], axis=2).reshape(P, -1)
        dn = i["ffn_w_down"][l, f].reshape(2, KF // 2, P, 4, 2, P)
        dn = dn.transpose(2, 3, 0, 4, 1, 5).reshape(P, -1)
        if f == 0:
            w = i["w_in"][l]
            a = w[:, 0:1536]
            b = w[:, 1568:]
            pa, pb = _units(i["w_pa"][l], P), _units(i["w_pb"][l], P)
            mix = [_units(a[:, 0:1024], P), _units(b[:, 0:512], P), _units(b[:, 512:768], P), _units(a[:, 1024:1536], P),
                   _units(b[:, 768:], P), pa[:, 0:2048], pa[:, 2048:], pb[:, 0:2048], pb[:, 2048:], _units(i["w_out"][l], P)]
            parts += [gu, dn] + mix
        else:
            parts += [gu, dn]
    return np.concatenate(parts, axis=1)


def _constants():
    c = np.zeros((P, C_ALL), np.float32)
    c[:, C_ID:C_ID + P] = np.eye(P)
    c[:, C_ONE:C_ONE + P] = 1
    j, i = np.arange(P)[:, None], np.arange(P)[None, :]
    same = j // CHUNK == i // CHUNK
    c[:, C_BLK:C_BLK + P] = same
    c[:, C_CUM[0]:C_CUM[0] + P] = (same & (j <= i)) / 16.0
    c[:, C_CUM[1]:C_CUM[1] + P] = (same & (j >= i)) / 16.0
    c[:, C_END[0]:C_END[0] + P] = (same & (j > i)) / 16.0
    c[:, C_END[1]:C_END[1] + P] = (same & (j < i)) / 16.0
    rot = np.zeros((P, P), np.float32)
    for s in range(0, P, 32):
        for q in range(16):
            rot[s + q, s + q + 16] = -1
            rot[s + q + 16, s + q] = 1
    c[:, C_ROT:C_ROT + P] = rot.T
    for g in range(2):
        dup = np.zeros((P, P), np.float32)
        for q in range(P):
            dup[q, 64 * g + q % 64] = 1
        c[:, C_DUP[g]:C_DUP[g] + P] = dup.T
        c[:, C_DROT[g]:C_DROT[g] + P] = (dup @ rot).T
    f32 = np.float32
    row, col = np.repeat(np.arange(SEQ // 64), 64).astype(f32), np.tile(np.arange(64), SEQ // 64).astype(f32)
    inv = (f32(10000.0) ** (-np.arange(0, 32, 2, dtype=f32) / f32(32))).astype(f32)
    ang = np.concatenate([row[:, None] * inv, col[:, None] * inv], axis=-1)
    ang = np.concatenate([np.zeros((META, 32), f32), ang], axis=0)
    d = np.arange(P) % 64
    which = (d // 32) * 16 + d % 16
    c[:, C_COS:C_COS + T] = np.cos(ang).T[which]
    c[:, C_SIN:C_SIN + T] = np.sin(ang).T[which]
    r32 = np.zeros((32, 32), np.float32)
    for q in range(16):
        r32[q, q + 16] = -1
        r32[q + 16, q] = 1
    c[0:32, C_R32:C_R32 + 32] = c[64:96, C_R32:C_R32 + 32] = r32.T
    inv2 = (f32(10000.0) ** (-np.arange(0, 32, 2, dtype=f32) / f32(32))).astype(f32)
    c[64:96, C_INV] = np.concatenate([inv2, inv2])
    m = np.where(j >= i, 0.0, np.finfo(np.float32).min)
    c[:, C_MASK:C_MASK + P] = m
    c[:, C_MASK + 2 * P:C_MASK + 3 * P] = m
    t = np.arange(16)
    for g, w in enumerate(POOL_W):
        c[:, C_CNT + 16 * g:C_CNT + 16 * g + 16] = 1.0 / np.minimum(t + 1, w)
    c[:, C_EPS] = EPS
    k = np.zeros((P, 2, T), np.int32)
    for c0, n in TILES:
        jj, ii = np.arange(n)[:, None], np.arange(n)[None, :]
        s = jj // CHUNK == ii // CHUNK
        k[0:n, 0, c0:c0 + n] = s & (jj <= ii)
        k[0:n, 1, c0:c0 + n] = s & (jj >= ii)
    return c, k.reshape(P, 2 * T)


def _layout(inp):
    i = {k: np.asarray(v) for k, v in inp.items()}
    f = {}
    h = np.concatenate([i["meta_tokens"], i["x"][0]], axis=0)
    f["x0"] = h.T.reshape(KD, P, T).transpose(1, 0, 2).reshape(P, KD * T)
    f["w1"] = np.stack([_layer1_weights(i, l) for l in range(L)])
    w2 = np.zeros((L, 33, 512), np.float32)
    w2[:, 0:16, 0:256] = i["gla_w2"][:, 0]
    w2[:, 16:32, 256:512] = i["gla_w2"][:, 1]
    w2[:, 32, :] = i["gla_b2"].reshape(L, 512)
    f["w2cat"] = w2
    f["lr_w"] = np.stack([_units(i["w_in"][l][:, 1536:1568], 32) for l in range(L)])
    f["vec1"] = np.stack([np.concatenate([
        _columns(i["norm_gains"][l].reshape(-1)), _columns(i["b_merge"][l].reshape(-1)), _columns(i["gla_gn"][l]),
        np.concatenate([i["q_norm"][l]] * 2)[:, None], np.concatenate([i["k_norm"][l]] * 2)[:, None]], axis=1) for l in range(L)])
    f["vecg"] = np.concatenate([_columns(i["final_norm"]), _columns(i["final_g_2"]), _columns(i["c_2"][0])], axis=1)
    a = i["w_ada_2"].reshape(L, 2, 4, P, 12, 512).transpose(0, 3, 1, 4, 2, 5)
    f["ada_w"] = a.reshape(L, P, 24 * 2048)
    f["b_ada"] = np.stack([_columns(i["b_ada_2"][l]) for l in range(L)])
    f["w2"], f["vec2"] = _layer2(i)
    f["pos"] = np.broadcast_to(i["positions_2"], (32, SEQ))
    f["const"], f["masks"] = _constants()
    return {k: np.ascontiguousarray(v) for k, v in f.items()}


def _layer2(i):
    ws, vs = [], []
    for l in range(L):
        w = i["w_in_2"][l]
        uq = i["w_uq_2"][l].reshape(QL, MH * QK)
        uk = i["w_uk_2"][l].reshape(KVL, 512)
        uv = i["w_uv_2"][l].reshape(KVL, 512)
        pp, pa = _units(i["p_pool_2"][l], P), _units(i["p_attn_2"][l], P)
        parts = [_units(w[:, 512:1152], P), _units(w[:, 1152:1184], 32), _units(w[:, 0:512], P), _units(uq, QK),
                 _units(uk, 64), _units(uv, 512), _units(w[:, 1184:], P),
                 i["w_pool_2"][l].transpose(1, 0, 2).reshape(P, 512),
                 pp[:, 0:2048], pa[:, 0:2048], pp[:, 2048:], pa[:, 2048:], _units(i["w_out_2"][l], P),
                 _units(i["w_ff1_2"][l], P)]
        f2 = i["w_ff2_2"][l].reshape(4, 8, P, 4, 2, P).transpose(2, 3, 0, 4, 1, 5).reshape(P, -1)
        ws.append(np.concatenate(parts + [f2], axis=1))
        vs.append(np.concatenate([_columns(i["ln1_g_2"][l]), _columns(i["ln2_g_2"][l]), _columns(i["q_norm_g_2"][l]),
                                  _columns(i["kv_norm_g_2"][l]), _columns(i["pool_scale_2"][l])], axis=1))
    return np.stack(ws), np.stack(vs)


_NAMES = ["x0", "w1", "w2cat", "lr_w", "vec1", "w2", "vec2", "vecg", "ada_w", "b_ada", "pos", "const", "masks"]


def kernel(**inputs):
    import concourse.bacc as bacc
    from concourse.bass_utils import run_bass_kernel_spmd

    nc = bacc.Bacc("TRN2", target_bir_lowering=False, num_devices=1)
    laid = _layout(inputs)
    arrays, args = {}, {}
    for name in _NAMES:
        a = laid[name]
        arrays[f"in_{name}"] = a
        args[name] = nc.dram_tensor(f"in_{name}", a.shape, mybir.dt.from_np(a.dtype), kind="ExternalInput").ap()
    args["out"] = nc.dram_tensor("out_0", (P, KD, SEQ), F32, kind="ExternalOutput").ap()
    program(nc, **args)
    r = run_bass_kernel_spmd(nc, [arrays], core_ids=[0])
    y = r.results[0]["out_0"]
    return y.transpose(2, 1, 0).reshape(1, SEQ, D)
```

```python
from contextlib import ExitStack

import numpy as np

import concourse.bass as bass
from concourse import mybir

F32 = mybir.dt.float32
F32R = mybir.dt.float32r
I32 = mybir.dt.int32
ACT = mybir.ActivationFunctionType
ALU = mybir.AluOpType
AX = mybir.AxisListType.X

P = 128
L = 2
D = 1024
KD = D // P
META = 16
SEQ = 256
T = META + SEQ
EPS = 1e-6

FF = 2816
FG = FF // 256
KF = FF // P
GLA_H, GLA_DK, GLA_DV, CHUNK = 4, 64, 128, 64
TILES = [(0, META), (META, P), (META + P, P)]
CHUNKS = [(0, 0, META)] + [(1 + i // 2, 64 * (i % 2), CHUNK) for i in range(4)]
CHUNK_COL = [0, 16, 80, 144, 208]
HD = 64

FF2 = 4096
KF2 = FF2 // P
MH, NOPE, ROPE = 8, 64, 32
QK = NOPE + ROPE
QL, KVL = 384, 256
POOL_W = (2, 4, 8, 16)
N_MOD = 6

GU_W, DN_W = 2048, 2816
FFN_W = FG * 2 * GU_W + 4 * 2 * DN_W
MIX1 = 25
W1_FFN = [0, FFN_W + MIX1 * 2048]
W1_MIX = FFN_W
W1_ALL = 2 * FFN_W + MIX1 * 2048
M2_WIDTH = [2048, 2048, 1280, 2048, 2048, 2304, 2048] + [2048] * 7 + [512] + [2048] * 9
M2_OFF = [sum(M2_WIDTH[:i]) for i in range(len(M2_WIDTH) + 1)]
W2_FF1 = M2_OFF[-1]
W2_FF2 = W2_FF1 + 16 * 2048
W2_ALL = W2_FF2 + 16 * 2048
ADA_N = N_MOD * D
RAW_W, UNIT_W = 2816, 1408
W2_AT = L * W1_ALL
FIRST_W = 2048
LN_EXP_SET, SILU_SET = 6, 18

C_ID, C_ONE, C_INV, C_EPS = 0, 128, 256, 257
C_FIRST = 258
C_BLK = C_FIRST
C_CUM, C_END = [C_BLK + P, C_BLK + 2 * P], [C_BLK + 3 * P, C_BLK + 4 * P]
C_ROT, C_DUP = C_BLK + 5 * P, [C_BLK + 6 * P, C_BLK + 7 * P]
C_DROT = [C_BLK + 8 * P, C_BLK + 9 * P]
C_COS = C_BLK + 10 * P
C_SIN = C_COS + T
C_R32 = C_SIN + T
C_MASK = C_R32 + 32
C_CNT = C_MASK + 384
C_ALL = C_CNT + 64

V_GAIN, V_BM, V_GN, V_QN, V_KN, V1_ALL = 0, 24, 40, 44, 45, 46
V_LN1, V_LN2, V_QG, V_KVG, V_PS, V2_ALL = 0, 8, 16, 19, 21, 25
G_FN, G_FG, G_C, G_ALL = 0, 8, 16, 24


class Event:

    def __init__(self, line, value):
        self.line, self.value = line, value


class Counts:

    def __init__(self, nc, ctx):
        self.nc = nc
        self.engine = {"pe": nc.tensor, "act": nc.scalar, "dve": nc.vector, "pool": nc.gpsimd, "sp": nc.sync}
        lines = ["pe", "act", "dve", "pool", "rawA", "rawB", "small", "vec", "ada"]
        self.sem = {n: ctx.enter_context(nc.semaphore(f"{n}_done")) for n in lines}
        self.out_sem = ctx.enter_context(nc.semaphore("out_done"))
        self.reset()

    def reset(self):
        self.count = {n: 0 for n in self.sem}
        self.seen = {}
        self.loop = None
        self.made = []

    def done(self, line, ins, by=1):
        ins.then_inc(self.sem[line], by)
        self.count[line] += by
        e = Event(line, self.count[line])
        self.made.append(e)
        return e

    def need(self, engine, *events):
        want = {}
        for e in events:
            if e is None:
                continue
            if isinstance(e, (list, tuple)):
                for x in e:
                    if x is not None:
                        want[x.line] = max(want.get(x.line, 0), x.value)
            else:
                want[e.line] = max(want.get(e.line, 0), e.value)
        for line, value in want.items():
            if self.seen.get((engine, line), 0) >= value:
                continue
            self.seen[engine, line] = value
            if self.loop and value > self.loop["base"][line]:
                value = value + self.loop["reg"] * self.loop["stride"][line]
            self.engine[engine].wait_ge(self.sem[line], value)

    def repeat(self, n, body):
        base = dict(self.count)
        body(0)
        mid = dict(self.count)
        stride = {k: mid[k] - base[k] for k in mid}
        self.made = []
        with self.nc.Fori(0, n - 2) as reg:
            self.loop = {"base": base, "stride": stride, "reg": reg}
            self.seen = {}
            body(reg + 1)
            assert all(self.count[k] - mid[k] == stride[k] for k in mid)
        self.loop = None
        self.seen = {}
        for e in self.made:
            e.value += (n - 3) * stride[e.line]
        for k in self.count:
            self.count[k] += (n - 3) * stride[k]
        body(n - 1)

    def new_layer(self):
        self.nc.all_engine_barrier()
        for n in self.sem:
            self.nc.gpsimd.sem_clear(self.sem[n])
        self.nc.all_engine_barrier()
        self.reset()


def program(nc, x0, weights, w2cat, lr_w, vec1, vec2, vecg, ada_w, b_ada, pos, const, masks, out):
    with ExitStack() as ctx:
        place = [nc.sbuf_base, nc.sbuf_top]

        def sb(name, shape, dt=F32):
            at = (place[0] + 63) // 64 * 64
            place[0] = at + 4 * int(np.prod(shape[1:]))
            assert place[0] <= place[1], (name, place)
            return nc.alloc_sbuf_tensor_at(name, shape, dt, offset=at)

        ct = Counts(nc, ctx)
        done, need = ct.done, ct.need
        pe, act, dve, pool, sp = nc.tensor, nc.scalar, nc.vector, nc.gpsimd, nc.sync
        bank = [ctx.enter_context(nc.psum_tensor(f"bank{i}", [P, 512], F32)) for i in range(8)]
        bank_free = [None] * 8

        x = sb("x", [P, KD, T])
        xn_hi = sb("xn_hi", [P, KD, T], F32R)
        xn_lo = sb("xn_lo", [P, KD, T], F32R)
        sumsq = sb("sumsq", [P, T])
        sq = sb("sq", [P, T])
        sq2 = sb("sq2", [P, T])
        rstd = sb("rstd", [P, T])
        full = sb("full", [P, 2, T])
        gate = sb("gate", [P, 2, T])
        raw = [sb("rawA", [P, RAW_W]), sb("rawB", [P, RAW_W])]
        w_hi = [sb(f"w_hi{u}", [P, UNIT_W], F32R) for u in range(4)]
        w_lo = [sb(f"w_lo{u}", [P, UNIT_W], F32R) for u in range(4)]
        cst = sb("cst", [P, C_ALL])
        vg = sb("vg", [P, G_ALL])
        c_act = sb("c_act", [P, KD])
        mod_all = sb("mod_all", [P, L, 48])

        ident = cst[:, C_ID:C_ID + P]
        ones = cst[:, C_ONE:C_ONE + P]
        eps = cst[:, C_EPS:C_EPS + 1]

        def A(ins):
            return done("act", ins)

        def V(ins):
            return done("dve", ins)

        def M(ins):
            return done("pe", ins)

        def G(ins):
            return done("pool", ins)

        def evacuated(b, *events):
            bank_free[b] = list(events)

        class Stream:
            landed = [None, None]
            hi_of = [None] * 4
            split_of = [None] * 4
            unit_free = [None] * 4
            raw_users = [[], []]

        S = Stream()

        def load(slot, src):
            need("sp", S.raw_users[slot])
            S.raw_users[slot] = []
            w = src.shape[1]
            S.landed[slot] = done(("rawA", "rawB")[slot], sp.dma_start(raw[slot][:, 0:w], src), 16)

        def split_hi(pair, u):
            if pair is None or pair.width[u] == 0:
                return
            slot, w = u // 2, pair.width[u]
            at = pair.width[2 * slot] if u % 2 else 0
            need("act", S.landed[slot], S.unit_free[u])
            S.hi_of[u] = A(act.activation(w_hi[u][:, 0:w], raw[slot][:, at:at + w], ACT.Copy))

        def split_lo(pair, u):
            if pair is None or pair.width[u] == 0:
                return
            slot, w = u // 2, pair.width[u]
            at = pair.width[2 * slot] if u % 2 else 0
            need("dve", S.landed[slot], S.unit_free[u], S.hi_of[u])
            v = V(dve.tensor_tensor(w_lo[u][:, 0:w], raw[slot][:, at:at + w], w_hi[u][:, 0:w].bitcast(F32), ALU.subtract))
            S.split_of[u] = [S.hi_of[u], v]
            S.raw_users[slot] += [v]

        def split(pair, u):
            split_hi(pair, u)
            split_lo(pair, u)

        class Pair:

            def __init__(self, src, width, work, post, lead=None):
                self.src, self.width, self.work, self.post, self.lead = src, width, work, post, lead

        def load_pair(pair):
            for slot in (0, 1):
                if pair.src[slot] is not None:
                    load(slot, pair.src[slot])

        def finish(chains):
            for g in chains:
                for _ in g:
                    pass

        def run_pair(cur, nxt, sides=(), at=0, aside=None, lead=False, hold=False):
            if nxt is not None:
                load_pair(nxt)
            if aside is not None:
                aside[0]()
            for u in range(4):
                finish([g for _, end, g in sides if end == at + u])
                if lead and u == cur.lead[0]:
                    cur.lead[1]()
                elif cur.work[u] is not None and not (lead and u == cur.lead[0] + 1):
                    need("pe", S.split_of[u])
                    w = cur.width[u]
                    S.unit_free[u] = M(cur.work[u](w_hi[u][:, 0:w], w_lo[u][:, 0:w]))
                rest = None
                if cur.work[u] is not None and cur.post[u] is not None:
                    rest = cur.post[u](S.unit_free[u])
                for begin, _, g in sides:
                    if at + u >= begin:
                        next(g, None)
                if not (hold and u >= 2):
                    split(nxt, u)
                if rest is not None:
                    rest()
                if aside is not None and u == aside[1]:
                    aside[2]()

        def product(o, wh, wl, xh, xl, first, last, lo_ready=None):
            pe.matmul(o, wh, xh, start=first, stop=False)
            pe.matmul(o, wl, xh, start=False, stop=False)
            need("pe", lo_ready)
            return pe.matmul(o, wh, xl, start=False, stop=last)

        def inverse_root(dst, src, scale, *waits):
            need("act", *waits)
            e = A(act.activation(dst, src, ACT.Ln, bias=eps, scale=scale))
            need("act", e)
            return A(act.activation(dst, dst, ACT.Exp, scale=-0.5))

        def load_table(table_set):
            act.add_instruction(mybir.InstLoadActFuncSet(name=nc.get_next_instruction_name(), act_func_set_id=table_set))

        def load_log_table():
            load_table(LN_EXP_SET)

        def all_so_far():
            return [Event(line, ct.count[line]) for line in ("pe", "act", "dve", "pool", "ada")]

        sq_free = [None, None]
        sumsq_free = [None]
        xn_ready = [None] * KD
        xn_free = [None]
        full_free = [[], []]

        def clear_sumsq():
            need("dve", sumsq_free[0])
            sumsq_free[0] = V(dve.memset(sumsq[:, :], 0.0))

        def add_squares(xk, ev, cols):
            n = xk.shape[-1]
            need("dve", ev, sq_free[0])
            v = V(dve.tensor_tensor(sq[:, 0:n], xk, xk, ALU.mult))
            need("dve", v, sumsq_free[0])
            v = V(dve.tensor_tensor(sumsq[:, cols], sumsq[:, cols], sq[:, 0:n], ALU.add))
            sq_free[0] = sumsq_free[0] = v

        def normalise(cols, gain, bias=None, b=7, into=None, held=None, gain_ready=None):
            need("pe", sumsq_free[0], bank_free[b])
            n = cols.stop - cols.start
            m = M(pe.matmul(bank[b][:, 0:n], ones, sumsq[:, cols], start=True, stop=True))
            r = inverse_root(rstd[:, cols], bank[b][:, 0:n], 1.0 / D, m)
            evacuated(b, r)
            sumsq_free[0] = m
            need("act", gain_ready)
            need("dve", gain_ready)
            lo_cols = slice(0, n)
            ready = [None] * KD

            def scaled(k):
                f = full[:, k % 2, 0:n]
                need("dve", r, full_free[k % 2])
                ready[k] = V(dve.scalar_tensor_tensor(out=f, in0=x[:, k, cols], scalar=gain[:, k:k + 1], in1=rstd[:, cols],
                                                      op0=ALU.mult, op1=ALU.mult))

            if into is None:
                scaled(0)
            else:
                need("dve", r)
            for k in range(KD):
                j = k % 2
                f, hi, lo = full[:, j, 0:n], xn_hi[:, k, lo_cols], xn_lo[:, k, lo_cols]
                if into is not None:
                    into(k, V(dve.scalar_tensor_tensor(out=x[:, k, cols], in0=x[:, k, cols], scalar=gain[:, k:k + 1],
                                                       in1=rstd[:, cols], op0=ALU.mult, op1=ALU.mult)))
                    continue
                need("act", ready[k], xn_free[0])
                if bias is None:
                    a = A(act.activation(hi, f, ACT.Copy))
                else:
                    a = A(act.activation(hi, f, ACT.Identity, bias=bias[:, k:k + 1]))
                if k + 1 < KD:
                    scaled(k + 1)
                need("dve", a, xn_free[0])
                if bias is None:
                    v = V(dve.tensor_tensor(lo, f, hi.bitcast(F32), ALU.subtract))
                else:
                    v = V(dve.scalar_tensor_tensor(out=lo, in0=f, scalar=bias[:, k:k + 1], in1=hi.bitcast(F32),
                                                   op0=ALU.add, op1=ALU.subtract))
                full_free[j] = [a, v]
                xn_ready[k] = [a, v]
                if k in (3, 5):
                    split_hi(held, 2 + k // 5)
            if into is None:
                split_lo(held, 2)
                split_lo(held, 3)

        def split_rows(hi, lo, src, *waits):
            need("act", *waits)
            a = A(act.activation(hi, src, ACT.Copy))
            need("dve", a, *waits)
            v = V(dve.tensor_tensor(lo, src, hi.bitcast(F32), ALU.subtract))
            return [a, v]

        def feature_tile(b, rows, n, k_tiles, xh, xl, ready, step=P):
            def work(wh, wl):
                need("pe", bank_free[b])
                for k in range(k_tiles):
                    need("pe", ready[k])
                    s = slice(k * step, k * step + rows)
                    o = bank[b][0:rows, 0:n]
                    m = product(o, wh[:, s], wl[:, s], xh[:, k, 0:n], xl[:, k, 0:n], k == 0, k == k_tiles - 1)
                return m
            return work

        def side_by_side(u0, n, xh, xl, ready):
            def work():
                need("pe", S.split_of[u0], S.split_of[u0 + 1], bank_free[0], bank_free[1])
                for k in range(KD):
                    need("pe", ready[k][0])
                    for b in range(2):
                        s = slice(k * P, (k + 1) * P)
                        m = product(bank[b][:, 0:n], w_hi[u0 + b][:, s], w_lo[u0 + b][:, s], xh[:, k, 0:n], xl[:, k, 0:n],
                                    k == 0, k == KD - 1, lo_ready=ready[k])
                        if k == KD - 1:
                            S.unit_free[u0 + b] = M(m)
            return u0, work

        def first_pair(at):
            return Pair([weights[:, bass.ds(at, FIRST_W)], weights[:, bass.ds(at + FIRST_W, FIRST_W)]], [FIRST_W // 2] * 4, None, None)

        def add_square_on_pe(k, cols, b, *waits):
            n = cols.stop - cols.start
            buf, j = (sq, sq2)[k % 2], k % 2
            need("act", sq_free[j], *waits)
            a = A(act.activation(buf[:, 0:n], x[:, k, cols], ACT.Square))
            need("pe", a)
            sq_free[j] = M(pe.matmul(bank[b][:, 0:n], ones, buf[:, 0:n], start=k == 0, stop=k == KD - 1))

        def keep_sumsq(cols, b):
            need("act", sq_free[(KD - 1) % 2])
            A(act.activation(sumsq[:, cols], bank[b][:, 0:cols.stop - cols.start], ACT.Copy, scale=1.0 / P))

        def fresh_layer():
            for i in range(8):
                bank_free[i] = None
            S.landed, S.split_of, S.unit_free, S.raw_users = [None] * 2, [None] * 4, [None] * 4, [[], []]
            S.hi_of = [None] * 4
            sq_free[0] = sq_free[1] = sumsq_free[0] = xn_free[0] = None
            full_free[0], full_free[1] = [], []

        TA, TB = slice(0, T), slice(META, T)
        N = SEQ
        RP = slice(64, 96)
        cos2 = sb("cos2", [96, N])
        sin2 = sb("sin2", [96, N])
        block_start = place[0]
        place[0] = place[1] - 16 * N - 64
        angle = sb("angle", [96, N])
        turns = sb("turns", [96, N])
        rest = sb("rest", [96, N])
        posi = sb("posi", [96, N], I32)
        place[0] = block_start

        def rope_angles():
            two_pi = 2 * np.pi
            c1 = 6.28125
            c2 = float(np.float32(np.floor((two_pi - c1) * 2 ** 20) / 2 ** 20))
            c3 = float(np.float32(two_pi - c1 - c2))
            magic = float(1.5 * 2 ** 23)

            def step(ins):
                v = V(ins)
                need("dve", v)
                return v
            step(dve.tensor_copy(rest[RP, :], posi[RP, :]))
            step(dve.tensor_scalar(angle[RP, :], rest[RP, :], cst[RP, C_INV:C_INV + 1], None, ALU.mult))
            step(dve.tensor_scalar(turns[RP, :], angle[RP, :], 1.0 / two_pi, magic, ALU.mult, ALU.add))
            step(dve.tensor_scalar(turns[RP, :], turns[RP, :], -magic, None, ALU.add))
            for c in (c1, c2, c3):
                step(dve.scalar_tensor_tensor(out=angle[RP, :], in0=turns[RP, :], scalar=-c, in1=angle[RP, :],
                                              op0=ALU.mult, op1=ALU.add))
            step(dve.tensor_scalar(rest[RP, :], angle[RP, :], np.pi / 2, None, ALU.add))
            step(dve.tensor_scalar(turns[RP, :], rest[RP, :], np.pi, None, ALU.is_gt))
            step(dve.scalar_tensor_tensor(out=rest[RP, :], in0=turns[RP, :], scalar=-two_pi, in1=rest[RP, :],
                                          op0=ALU.mult, op1=ALU.add))
            top = float(np.nextafter(np.float32(np.pi), np.float32(0)))
            for buf in (angle, rest):
                v = step(dve.tensor_scalar(buf[RP, :], buf[RP, :], top, -top, ALU.min, ALU.max))
            return v

        done("small", sp.dma_start(x[:, :, :], x0.rearrange("p (k t) -> p k t", k=KD)), 16)
        done("small", sp.dma_start(cst[:, 0:C_FIRST], const[:, 0:C_FIRST]), 16)
        done("small", sp.dma_start(vg[:, :], vecg), 16)
        e_first = done("small", sp.dma_start(posi[RP, :], pos), 16)
        ahead = first_pair(0)
        load(0, ahead.src[0])
        done("vec", sp.dma_start(cst[:, C_FIRST:], const[:, C_FIRST:]), 16)
        load(1, ahead.src[1])
        need("act", e_first)
        need("dve", e_first)
        need("pe", e_first)
        for k in range(KD):
            add_square_on_pe(k, TA, 7)
        keep_sumsq(TA, 7)
        A(act.activation(c_act[:, :], vg[:, G_C:G_C + KD], ACT.Silu))
        angles = rope_angles()
        split(ahead, 0)
        split(ahead, 1)
        need("act", angles)
        A(act.activation(sin2[RP, :], angle[RP, :], ACT.Sin))
        A(act.activation(cos2[RP, :], rest[RP, :], ACT.Sin))
        need("act", S.landed[1])

        v1 = sb("v1", [P, V1_ALL])
        bada = sb("bada", [P, 48])
        att = [sb(f"att{i}", [P, T]) for i in range(4)]
        msk = sb("msk", [P, 2, T], I32)
        shared_start = place[0]
        h_hi = sb("h_hi", [P, KF, T], F32R)
        h_lo = sb("h_lo", [P, KF, T], F32R)
        acc = sb("acc", [P, ADA_N])
        ada_raw = sb("ada_raw", [P, 2048])
        ffn_end = place[0]
        place[0] = shared_start
        qa = sb("qa", [P, 2, T])
        ka = sb("ka", [P, 2, T])
        vtok = sb("vtok", [P, 3, 512])
        r_act = sb("r_act", [P, 4, T])
        qb = sb("qb", [P, 4, T])
        kb = sb("kb", [P, T])
        kdup = sb("kdup", [P, 2, T])
        vb = sb("vb", [P, 3, P])
        qdec = sb("qdec", [P, 4, T])
        kinv = sb("kinv", [P, 4, T])
        states = sb("states", [P, 4, 4, P])
        decay = sb("decay", [P, 4, 5])
        gates = sb("gates", [P, 16, T])
        b_hi = sb("b_hi", [P, 4, T], F32R)
        b_lo = sb("b_lo", [P, 4, T], F32R)
        stat = sb("stat", [P, 16])
        qb_meta = sb("qb_meta", [P, 4, META])
        reused = place[0]
        la = sb("la", [P, 3, 512])
        e_cum = sb("e_cum", [P, 2, T])
        kend_t = sb("kend_t", [P, 2, 3, P])
        end_la = place[0]
        place[0] = reused
        a_hi = sb("a_hi", [P, 4, T], F32R)
        a_lo = sb("a_lo", [P, 4, T], F32R)
        place[0] = reused = max(place[0], end_la, ffn_end)
        lr_raw = sb("lr_raw", [P, 256])
        lr_hi = sb("lr_hi", [P, 256], F32R)
        lr_lo = sb("lr_lo", [P, 256], F32R)
        w2c = sb("w2c", [33, 512])
        lrT = sb("lrT", [33, T])
        place[0] = reused
        prob = sb("prob", [P, 2, T])
        pt = sb("pt", [P, 2, 3, SEQ])
        lt = sb("lt", [P, 3, P])
        y_hi, y_lo = xn_hi, xn_lo

        for a4 in att:
            G(pool.memset(a4[:, :], 0.0))
        e_rest = done("vec", sp.dma_start(msk[:, :, :], masks.rearrange("p (d t) -> p d t", d=2)), 16)
        need("pool", e_rest)

        def layer1(l):
            fresh_layer()
            small = done("vec", sp.dma_start(v1[:, :], vec1[l]), 16)
            small = done("vec", sp.dma_start(bada[:, :], b_ada[l]), 16)
            ada = {"landed": None, "used": None}

            def ada_load(f, j, waits=None):
                need("sp", ada["used"], waits)
                ada["landed"] = done("ada", sp.dma_start(
                    ada_raw[:, :], ada_w[l, :, bass.ds((f * 12 + j) * 2048, 2048)] if not isinstance(j, int)
                    else ada_w[l, :, (f * 12 + j) * 2048:(f * 12 + j + 1) * 2048]), 16)

            def ada_piece(f, j):
                o = acc[:, bass.ds(j * 512, 512)]
                need("dve", ada["landed"])
                for i in range(4):
                    w, c = ada_raw[:, i * 512:(i + 1) * 512], c_act[:, 4 * f + i:4 * f + i + 1]
                    if i == 0:
                        v = V(dve.tensor_scalar(o, w, c, None, ALU.mult))
                    else:
                        v = V(dve.scalar_tensor_tensor(out=o, in0=w, scalar=c, in1=o, op0=ALU.mult, op1=ALU.add))
                    need("dve", v)
                ada["used"] = v

            def reduce_ada(f):
                need("pe", ada["used"], bank_free[0])
                for j in range(48):
                    if j == 44:
                        need("pe", ada["used"])
                    m = pe.matmul(bank[0][:, j:j + 1], acc[:, j * P:(j + 1) * P], ones[:, 0:1], start=True, stop=True)
                    if j in (14, 29, 43):
                        yield
                m = M(m)
                need("dve", m)
                mod = mod_all[:, bass.ds(l, 1), :]
                v = V(dve.tensor_tensor(mod, bank[0][:, 0:48].rearrange("p (a n) -> p a n", a=1),
                                        bada[:, :].rearrange("p (a n) -> p a n", a=1) if f == 0 else mod, ALU.add))
                evacuated(0, v)

            def w1_src(off, w, step=0, i=0):
                o = off + i * step
                return weights[:, bass.ds(o + l * W1_ALL, w)]

            ev = {}

            gate_free = [None, None]

            def gate_up(f, i):
                o = W1_FFN[f]
                src = [w1_src(o, GU_W, 2 * GU_W, i), w1_src(o + GU_W, GU_W, 2 * GU_W, i)]
                work = [feature_tile(b, P, T, KD, xn_hi, xn_lo, xn_ready) for b in range(4)]

                def gated(j):
                    def post(m):
                        need("act", m, gate_free[j])
                        g = A(act.activation(gate[:, j, :], bank[j][:, 0:T], ACT.Silu))
                        evacuated(j, g)
                        need("dve", m, g, full_free[j])
                        v = V(dve.tensor_tensor(full[:, j, :], gate[:, j, :], bank[2 + j][:, 0:T], ALU.mult))
                        gate_free[j] = v
                        evacuated(2 + j, v)
                        hh, hl = h_hi[:, bass.ds(2 * i + j, 1), :], h_lo[:, bass.ds(2 * i + j, 1), :]
                        fj = full[:, j:j + 1, :]
                        def rest():
                            full_free[j] = split_rows(hh, hl, fj, v)
                            if j == 0:
                                h_ready[0] = h_ready[1]
                            h_ready[1] = full_free[j]
                        return rest
                    return post
                return Pair(src, [1024] * 4, work, [None, None, gated(0), gated(1)], side_by_side(0, T, xn_hi, xn_lo, xn_ready))

            h_ready = [None, None]
            HK = KF // 2

            def down(f, g):
                o = W1_FFN[f] + FG * 2 * GU_W
                src = [w1_src(o, DN_W, 2 * DN_W, g), w1_src(o + DN_W, DN_W, 2 * DN_W, g)]

                def part(half, j):
                    def work(wh, wl):
                        b = 4 + j
                        if half == 0:
                            need("pe", bank_free[b])
                        need("pe", h_ready[half])
                        for k in range(HK):
                            s = slice(k * P, (k + 1) * P)
                            kk = half * HK + k
                            m = product(bank[b][:, 0:T], wh[:, s], wl[:, s], h_hi[:, kk, :], h_lo[:, kk, :],
                                        kk == 0, kk == KF - 1)
                        return m
                    return work

                def add(j):
                    def post(m):
                        xk = x[:, bass.ds(2 * g + j, 1), :]
                        need("dve", m)
                        v = V(dve.scalar_tensor_tensor(out=xk, in0=bank[4 + j][:, 0:T].rearrange("p (a t) -> p a t", a=1),
                                                       scalar=0.5, in1=xk, op0=ALU.mult, op1=ALU.add))
                        evacuated(4 + j, v)
                        add_squares(xk.rearrange("p a t -> p (a t)"), v, TA)
                    return post
                return Pair(src, [1408] * 4, [part(0, 0), part(0, 1), part(1, 0), part(1, 1)], [None, None, add(0), add(1)])

            def ffn(f, gain, nxt, gain_ready=None):
                before = all_so_far()
                normalise(TA, gain, held=gate_up(f, 0), gain_ready=gain_ready)
                clear_sumsq()
                load_table(SILU_SET)
                need("act", before)
                need("dve", before)

                def step(i):
                    last = isinstance(i, int) and i == FG - 1

                    run_pair(gate_up(f, i), down(f, 0) if last else gate_up(f, i + 1),
                             aside=(lambda: ada_load(f, i, before if isinstance(i, int) and i == 0 else None), 3, lambda: ada_piece(f, i)),
                             lead=isinstance(i, int) and i == 0)
                ct.repeat(FG, step)
                xn_free[0] = S.unit_free[3]

                def dstep(g):
                    last = isinstance(g, int) and g == 3
                    if last:
                        if f == 0:
                            split_low_rank()
                        load_log_table()
                    run_pair(down(f, g), nxt if last else down(f, g + 1), [(0, 4, reduce_ada(f))] if last else (), hold=last,
                             aside=(lambda: ada_load(f, FG), 2, lambda: ada_piece(f, FG)) if last else None)
                ct.repeat(4, dstep)

            a_ready, b_ready, y_ready = [None] * 4, [None] * 4, [None] * KD

            def mix_src(c):
                return w1_src(W1_MIX + 2048 * c, 2048)

            def copy_to(dst, b, key, scale=1.0, bias=None):
                def post(m):
                    need("act", m)
                    if bias is None:
                        e = A(act.activation(dst, bank[b][:, 0:T], ACT.Copy, scale=scale))
                    else:
                        e = A(act.activation(dst, bank[b][:, 0:T], ACT.Identity, bias=bias))
                    ev[key] = e
                    evacuated(b, e)
                return post

            def xtile(b):
                return feature_tile(b, P, T, KD, xn_hi, xn_lo, xn_ready)

            def token_tiles(bs, cols, width=P):
                def work(wh, wl):
                    for t, (c0, n) in enumerate(TILES):
                        b = bs[t]
                        need("pe", bank_free[b])
                        o = bank[b][0:n, cols[t]:cols[t] + width]
                        for k in range(KD):
                            need("pe", xn_ready[k])
                            s = slice(k * width, (k + 1) * width)
                            cs = slice(c0, c0 + n)
                            pe.matmul(o, xn_hi[:, k, cs], wh[:, s], start=k == 0, stop=False)
                            pe.matmul(o, xn_lo[:, k, cs], wh[:, s], start=False, stop=False)
                            m = pe.matmul(o, xn_hi[:, k, cs], wl[:, s], start=False, stop=k == KD - 1)
                    return m
                return work

            def values_part(u):
                def work(wh, wl):
                    for t, (c0, n) in enumerate(TILES):
                        b = 5 + t
                        need("pe", bank_free[b] if u == 0 else None)
                        cs = slice(c0, c0 + n)
                        for k in (2 * u, 2 * u + 1):
                            s = slice((k - 2 * u) * 512, (k - 2 * u + 1) * 512)
                            pe.matmul(bank[b][0:n, :], xn_hi[:, k, cs], wh[:, s], start=k == 0, stop=False)
                            pe.matmul(bank[b][0:n, :], xn_hi[:, k, cs], wl[:, s], start=False, stop=False)
                            m = pe.matmul(bank[b][0:n, :], xn_lo[:, k, cs], wh[:, s], start=False, stop=k == KD - 1)
                    return m
                return work

            def v_out(m):
                need("act", m)
                for t, (c0, n) in enumerate(TILES):
                    e = A(act.activation(vtok[0:n, t, :], bank[5 + t][0:n, :], ACT.Copy))
                    evacuated(5 + t, e)
                ev["v"] = e

            def vb_out(m):
                need("act", m)
                for t, (c0, n) in enumerate(TILES):
                    e = A(act.activation(vb[0:n, t, :], bank[1][0:n, t * P:(t + 1) * P], ACT.Copy))
                evacuated(1, e)
                ev["vb"] = e

            def gate_out_dve(j, b):
                def post(m):
                    need("dve", m)
                    v = V(dve.tensor_scalar(gates[:, j, :], bank[b][:, 0:T], v1[:, V_BM + j:V_BM + j + 1], None, ALU.add))
                    evacuated(b, v)
                    ev["g_dve", j] = v
                return post

            def gate_out(j, b):
                return copy_to(gates[:, j, :], b, ("g", j), bias=v1[:, V_BM + j:V_BM + j + 1])

            def load_low_rank():
                done("small", sp.dma_start(lr_raw[:, :], lr_w[l]), 16)
                ev["lr_landed"] = done("small", sp.dma_start(w2c[:, :], w2cat[l]), 16)

            def split_low_rank():
                ev["lr"] = split_rows(lr_hi[:, :], lr_lo[:, :], lr_raw[:, :], ev["lr_landed"])
                ev["lr"].append(V(dve.memset(lrT[32:33, :], 1.0)))

            def log_gates():
                need("pe", ev["lr"], bank_free[4])
                for k in range(KD):
                    need("pe", xn_ready[k])
                    ks = slice(32 * k, 32 * k + 32)
                    m = product(bank[4][0:32, 0:T], lr_hi[:, ks], lr_lo[:, ks], xn_hi[:, k, :], xn_lo[:, k, :], k == 0, k == KD - 1)
                m = M(m)
                need("act", m)
                e = A(act.activation(lrT[0:32, :], bank[4][0:32, 0:T], ACT.Copy))
                evacuated(4, e)
                yield
                need("pe", e)
                for t, (c0, n) in enumerate(TILES):
                    need("pe", bank_free[5 + t])
                    m = M(pe.matmul(bank[5 + t][0:n, :], lrT[0:33, c0:c0 + n], w2c[0:33, :], start=True, stop=True))
                    need("act", m)
                    e = A(act.activation(la[0:n, t, :], bank[5 + t][0:n, :], ACT.Abs))
                    need("act", e)
                    e = A(act.activation(la[0:n, t, :], la[0:n, t, :], ACT.Exp, scale=-1.0))
                    need("act", e)
                    e = A(act.activation(la[0:n, t, :], la[0:n, t, :], ACT.Ln, bias=ones[0:n, 0:1]))
                    need("dve", e)
                    v = V(dve.scalar_tensor_tensor(out=la[0:n, t, :], in0=bank[5 + t][0:n, :], scalar=0.0, in1=la[0:n, t, :],
                                                   op0=ALU.min, op1=ALU.subtract))
                    evacuated(5 + t, v)
                ev["la"] = v

            def gla():
                kt_free = [None, None]
                e_free = [None, None]
                for d in range(2):
                    for p in range(2):
                        i = 2 * d + p
                        need("pe", ev["la"])
                        for b, c in ((2, C_CUM[d]), (3, C_END[d])):
                            need("pe", bank_free[b])
                            for t, (c0, n) in enumerate(TILES):
                                m = pe.matmul(bank[b][:, c0:c0 + n], la[0:n, t, d * 256 + p * P:d * 256 + p * P + P],
                                              cst[0:n, c:c + n], start=True, stop=True)
                        m = M(m)
                        need("act", m, e_free[0], e_free[1])
                        e0 = A(act.activation(e_cum[:, 0, :], bank[2][:, 0:T], ACT.Exp))
                        e1 = A(act.activation(e_cum[:, 1, :], bank[2][:, 0:T], ACT.Exp, scale=-1.0))
                        evacuated(2, e1)
                        need("dve", e0, ev["qa", p])
                        V(dve.tensor_tensor(qdec[:, i, :], qa[:, p, :], e_cum[:, 0, :], ALU.mult))
                        for c in range(5):
                            cc = CHUNK_COL[c] + (CHUNKS[c][2] - 1 if d == 0 else 0)
                            v = V(dve.tensor_copy(decay[:, i, c:c + 1], e_cum[:, 0, cc:cc + 1]))
                        need("dve", e1, ev["ka", p])
                        v = V(dve.tensor_tensor(kinv[:, i, :], ka[:, p, :], e_cum[:, 1, :], ALU.mult))
                        need("act", v)
                        e2 = A(act.activation(e_cum[:, 0, :], bank[3][:, 0:T], ACT.Exp))
                        evacuated(3, e2)
                        need("dve", e2)
                        v = V(dve.tensor_tensor(e_cum[:, 1, :], ka[:, p, :], e_cum[:, 0, :], ALU.mult))
                        e_free[0] = v
                        yield
                        need("pe", v, bank_free[4])
                        for t, (c0, n) in enumerate(TILES):
                            m = pe.transpose(bank[4][0:n, t * P:(t + 1) * P], e_cum[:, 1, c0:c0 + n], ident)
                        m = M(m)
                        e_free[1] = m
                        j = i % 2
                        need("act", m, kt_free[j])
                        A(act.activation(kend_t[0:META, j, 0, :], bank[4][0:META, 0:P], ACT.Copy))
                        e = A(act.activation(kend_t[:, j, 1:3, :], bank[4][:, P:3 * P], ACT.Copy))
                        evacuated(4, e)
                        yield
                        need("pe", e, ev["v"], bank_free[2], bank_free[3])
                        order = [0, 1, 2, 3] if d == 0 else [4, 3, 2, 1]
                        for s, c in enumerate(order):
                            t, po, n = CHUNKS[c]
                            for hh in range(2):
                                h = 2 * p + hh
                                m = pe.matmul(bank[3 if po else 2][64 * hh:64 * hh + 64, s * P:(s + 1) * P],
                                              kend_t[po:po + n, j, t, 64 * hh:64 * hh + 64],
                                              vtok[po:po + n, t, h * P:(h + 1) * P], start=True, stop=True)
                        m = M(m)
                        kt_free[j] = m
                        need("dve", m)
                        v = V(dve.tensor_copy(states[:, i, 0, :], bank[3 if CHUNKS[order[0]][1] else 2][:, 0:P]))
                        for s in range(1, 4):
                            need("dve", v)
                            v = V(dve.scalar_tensor_tensor(out=states[:, i, s, :], in0=states[:, i, s - 1, :],
                                                           scalar=decay[:, i, order[s]:order[s] + 1],
                                                           in1=bank[3 if CHUNKS[order[s]][1] else 2][:, s * P:(s + 1) * P],
                                                           op0=ALU.mult, op1=ALU.add))
                        evacuated(2, v)
                        evacuated(3, v)
                        ev["state", i] = v
                        yield
                att_free = [None] * 4
                for h in range(GLA_H):
                    p, hr = h // 2, slice(64 * (h % 2), 64 * (h % 2) + 64)
                    for d in range(2):
                        i, b, o = 2 * d + p, 2 + d, att[2 * (h % 2) + d]
                        need("pe", ev["state", i], bank_free[b])
                        for t, (c0, n) in enumerate(TILES):
                            m = pe.matmul(bank[b][0:n, c0:c0 + n], kinv[hr, i, c0:c0 + n], qdec[hr, i, c0:c0 + n],
                                          start=True, stop=True)
                        m = M(m)
                        need("dve", m, att_free[2 * (h % 2) + d])
                        V(dve.copy_predicated(o[0:META, 0:META], msk[0:META, d, 0:META], bank[b][0:META, 0:META]))
                        v = V(dve.copy_predicated(o[:, META:T], msk[:, d, META:T], bank[b][:, META:T]))
                        evacuated(b, v)
                    yield
                    need("pe", v, bank_free[4])
                    for t, (c0, n) in enumerate(TILES):
                        vt = vtok[0:n, t, h * P:(h + 1) * P]
                        todo = []
                        for d in range(2):
                            i = 2 * d + p
                            todo.append((bank[4][:, c0:c0 + n], vt, att[2 * (h % 2) + d][0:n, c0:c0 + n]))
                            order = [0, 1, 2, 3] if d == 0 else [4, 3, 2, 1]
                            for s, c in enumerate([1, 2, 3, 4] if d == 0 else [3, 2, 1, 0]):
                                if CHUNKS[c][0] == t:
                                    cs = slice(CHUNK_COL[c], CHUNK_COL[c] + CHUNKS[c][2])
                                    todo.append((bank[4][:, cs], states[hr, i, s, :], qdec[hr, i, cs]))
                        todo.sort(key=lambda z: z[2].shape[0] != n)
                        for q, (o, lh, rh) in enumerate(todo):
                            m = pe.matmul(o, lh, rh, start=q == 0, stop=q == len(todo) - 1, skip_group_check=True)
                    m = M(m)
                    att_free[2 * (h % 2)] = att_free[2 * (h % 2) + 1] = m
                    need("act", m, sq_free[0])
                    a = A(act.activation(sq[:, :], bank[4][:, 0:T], ACT.Square))
                    yield
                    need("pe", a, bank_free[2])
                    m2 = M(pe.matmul(bank[2][:, 0:T], ones, sq[:, :], start=True, stop=True))
                    sq_free[0] = m2
                    r = inverse_root(gate[:, 0, :], bank[2][:, 0:T], 1.0 / GLA_DV, m2, gate_free[0])
                    evacuated(2, r)
                    need("dve", r, full_free[0])
                    v = V(dve.tensor_tensor(full[:, 0, :], bank[4][:, 0:T], gate[:, 0, :], ALU.mult))
                    gate_free[0] = v
                    evacuated(4, v)
                    need("dve", v, ev["silu_r"])
                    v = V(dve.scalar_tensor_tensor(out=full[:, 0, :], in0=full[:, 0, :], scalar=v1[:, V_GN + h:V_GN + h + 1],
                                                   in1=r_act[:, h, :], op0=ALU.mult, op1=ALU.mult))
                    a_ready[h] = split_rows(a_hi[:, h, :], a_lo[:, h, :], full[:, 0, :], v)
                    full_free[0] = a_ready[h]
                    yield

            def attention():
                bS, bT, bO = 5, 6, 7

                def tile(k):
                    return qb[:, k, :] if k < 4 else kb[:, :]

                def rotate(b, b2, turn_c, src_c, src, dst):
                    need("pe", scaled[0], bank_free[b], bank_free[b2] if src_c else None)
                    m = M(pe.matmul(bank[b][:, 0:T], cst[:, turn_c:turn_c + P], src, start=True, stop=True))
                    if src_c:
                        m = M(pe.matmul(bank[b2][:, 0:T], cst[:, src_c:src_c + P], src, start=True, stop=True))
                    need("dve", m, full_free[1])
                    v = V(dve.tensor_tensor(full[:, 1, :], bank[b][:, 0:T], cst[:, C_SIN:C_SIN + T], ALU.mult))
                    evacuated(b, v)
                    v = V(dve.tensor_tensor(dst, bank[b2][:, 0:T] if src_c else src, cst[:, C_COS:C_COS + T], ALU.mult))
                    if src_c:
                        evacuated(b2, v)
                    need("dve", v)
                    v = V(dve.tensor_tensor(dst, dst, full[:, 1, :], ALU.add))
                    full_free[1] = [v]
                    return v

                squared, scaled = None, [None]
                for j in range(7):
                    if j > 1:
                        if j - 2 < 4:
                            v = rotate(bT, None, C_ROT, None, tile(j - 2), tile(j - 2))
                            need("dve", v)
                            V(dve.tensor_copy(qb_meta[:, j - 2, :], qb[:, j - 2, 0:META]))
                        else:
                            for g in range(2):
                                v = rotate((bT, bS)[g], (bO, bO)[g], C_DROT[g], C_DUP[g], kb[:, :], kdup[:, g, :])
                            ev["rope"] = v
                    if 0 < j < 6:
                        k = j - 1
                        need("pe", squared, bank_free[bS])
                        m = M(pe.matmul(bank[bS][:, 0:T], cst[:, C_BLK:C_BLK + P], sq2[:, :], start=True, stop=True))
                        sq_free[1] = m
                        r = inverse_root(gate[:, 1, :], bank[bS][:, 0:T], 1.0 / HD, m, gate_free[1])
                        evacuated(bS, r)
                        need("dve", r)
                        g = V_QN if k < 4 else V_KN
                        v = V(dve.scalar_tensor_tensor(out=tile(k), in0=tile(k), scalar=v1[:, g:g + 1], in1=gate[:, 1, :],
                                                       op0=ALU.mult, op1=ALU.mult))
                        scaled[0] = gate_free[1] = v
                    if j < 5:
                        need("act", sq_free[1], ev["qb", j] if j < 4 else ev["kb"], ev["la"])
                        squared = A(act.activation(sq2[:, :], tile(j), ACT.Square))
                    yield
                prob_free = [None, None]
                st = [0]

                def softmax(b, j):
                    c = 4 * (st[0] % 4)
                    st[0] += 1
                    mx, nb, su, rc = (stat[:, c + i:c + i + 1] for i in range(4))
                    v = V(dve.reduce_max(mx, bank[b][:, 0:T], AX))
                    need("dve", v)
                    v = V(dve.tensor_scalar(nb, mx, -HD ** -0.5, None, ALU.mult))
                    need("act", v, prob_free[j])
                    a = A(act.activation(prob[:, j, :], bank[b][:, 0:T], ACT.Exp, bias=nb, scale=HD ** -0.5, accum_out=su))
                    evacuated(b, a)
                    need("dve", a)
                    v = V(dve.reciprocal(rc, su))
                    need("dve", v)
                    return V(dve.tensor_scalar(prob[:, j, :], prob[:, j, :], rc, None, ALU.mult))

                def turn(j, b, v, dst, dst0, *waits):
                    need("pe", v, bank_free[b])
                    for t, (c0, n) in enumerate(TILES):
                        m = pe.transpose(bank[b][0:n, t * P:(t + 1) * P], prob[:, j, c0:c0 + n], ident)
                    m = M(m)
                    prob_free[j] = m
                    need("act", m, *waits)
                    a = A(act.activation(dst0, bank[b][0:META, 0:P], ACT.Copy))
                    a2 = A(act.activation(dst, bank[b][:, P:3 * P].rearrange("p (t n) -> p t n", t=2), ACT.Copy))
                    evacuated(b, a2)
                    return a2

                need("pe", ev["rope"], bank_free[bS])
                for g in range(2):
                    for par in range(2):
                        r0 = 64 * g + 32 * par
                        hr = slice(64 * par, 64 * par + 64)
                        m = pe.matmul(bank[bS][r0:r0 + 32, 0:T], qb_meta[hr, 2 * g:2 * g + 2, :].rearrange("p a t -> p (a t)"),
                                      kdup[hr, g, :], start=True, stop=True)
                m = M(m)
                need("dve", m)
                turned = softmax(bS, 0)
                yield
                e_lt = turn(0, bT, turned, lt[:, 1:3, :], lt[0:META, 0, :])
                pt_free = [None, None]
                tiles = [(p, par, t) for p in range(4) for par in range(2) for t in (1, 2)]
                e_pt = None
                for i in range(len(tiles) + 2):
                    if i > 2 and i % 2:
                        p, par, _ = tiles[i - 3]
                        g = (2 * p + par) // 4
                        need("pe", e_pt, e_lt, ev["vb"], bank_free[bO] if par == 0 else None)
                        o = bank[bO][64 * par:64 * par + 64, :]
                        lc = 64 * g + 32 * par + 16 * (p % 2)
                        for t, (c0, n) in enumerate(TILES):
                            pe.matmul(o[:, META:T], vb[0:n, t, g * 64:g * 64 + 64], pt[0:n, par, t, :], start=t == 0, stop=t == 2)
                        for t, (c0, n) in enumerate(TILES):
                            m = pe.matmul(o[:, 0:META], vb[0:n, t, g * 64:g * 64 + 64], lt[0:n, t, lc:lc + META],
                                          start=t == 0, stop=t == 2)
                        m = M(m)
                        pt_free[par] = m
                        if par:
                            b_ready[p] = split_rows(b_hi[:, p, :], b_lo[:, p, :], bank[bO][:, 0:T], m)
                            evacuated(bO, *b_ready[p])
                    if 0 < i <= len(tiles):
                        _, par, t = tiles[i - 1]
                        e_pt = turn(t - 1, bT, turned, pt[:, par, 1:3, (t - 1) * P:t * P],
                                    pt[0:META, par, 0, (t - 1) * P:t * P], pt_free[par])
                    if i < len(tiles):
                        p, par, t = tiles[i]
                        hr = slice(64 * par, 64 * par + 64)
                        c0, n = TILES[t]
                        need("pe", bank_free[bS])
                        m = M(pe.matmul(bank[bS][:, 0:T], qb[hr, p, c0:c0 + n], kdup[hr, (2 * p + par) // 4, :], start=True, stop=True))
                        need("dve", m)
                        turned = softmax(bS, t - 1)
                    yield

            def r_out(j, b):
                def post(m):
                    need("act", m)
                    e = A(act.activation(r_act[:, j, :], bank[b][:, 0:T], ACT.Copy))
                    evacuated(b, e)
                    ev["r", j] = e
                    if j == 3:
                        need("act", e)
                        ev["silu_r"] = A(act.activation(r_act[:, :, :], r_act[:, :, :], ACT.Silu))
                        load_log_table()
                return post

            def half_tiles(bs, xh, xl, ready):
                def work(wh, wl):
                    for j, b in enumerate(bs):
                        need("pe", bank_free[b])
                        for k in range(4):
                            need("pe", ready[k])
                            s = slice((4 * j + k) * P, (4 * j + k + 1) * P)
                            m = product(bank[b][:, 0:T], wh[:, s], wl[:, s], xh[:, k, :], xl[:, k, :], k == 0, k == 3)
                    return m
                return work

            def merged_a(ms, bs):
                def post(m):
                    for mt, b in zip(ms, bs):
                        need("dve", m, ev["sig", 0])
                        v = V(dve.tensor_tensor(gates[:, mt, :], gates[:, mt, :], bank[b][:, 0:T], ALU.mult))
                        evacuated(b, v)
                        ev["ya", mt] = v
                return post

            def merged_b(ms, bs):
                def post(m):
                    for mt, b in zip(ms, bs):
                        need("dve", m, ev["ya", mt], ev["sig", 1])
                        v = V(dve.tensor_tensor(gates[:, 8 + mt, :], gates[:, 8 + mt, :], bank[b][:, 0:T], ALU.mult))
                        evacuated(b, v)
                    need("dve", v)
                    vs = [V(dve.tensor_tensor(gates[:, mt, :], gates[:, mt, :], gates[:, 8 + mt, :], ALU.add)) for mt in ms]

                    def rest():
                        for mt, v in zip(ms, vs):
                            y_ready[mt] = split_rows(y_hi[:, mt, :], y_lo[:, mt, :], gates[:, mt, :], v, xn_free[0])
                    return rest
                return post

            def mixed_out(mt, b):
                def post(m):
                    need("dve", m)
                    v = V(dve.tensor_tensor(x[:, mt, :], x[:, mt, :], bank[b][:, 0:T], ALU.add))
                    evacuated(b, v)
                    add_squares(x[:, mt, :], v, TA)
                return post

            def last_gate(m):
                gate_out(15, 1)(m)
                xn_free[0] = m
                gates_sigmoid(0)

            def gates_sigmoid(half):
                g = gates[:, 8 * half:8 * half + 8, :]
                need("act", ev["g", 15], ev["g_dve", 1])
                ev["sig", half] = A(act.activation(g, g, ACT.Sigmoid))
                if half:
                    load_log_table()

            def first_merged(m):
                merged_a([0, 1], [0, 1])(m)
                gates_sigmoid(1)

            def pair(c, works, posts, lead=None):
                n = len(works)
                return Pair([mix_src(c), mix_src(c + 1) if n == 4 else None], [1024] * n + [0] * (4 - n),
                            works + [None] * (4 - n), posts + [None] * (4 - n), lead)

            def ytile(b):
                return feature_tile(b, P, T, KD, y_hi, y_lo, y_ready)

            ab, cd = [0, 1], [2, 3]
            pairs = [
                pair(0, [xtile(0), xtile(1), xtile(2), xtile(3)],
                     [copy_to(qa[:, 0, :], 0, ("qa", 0), GLA_DK ** -0.5), copy_to(qa[:, 1, :], 1, ("qa", 1), GLA_DK ** -0.5),
                      copy_to(ka[:, 0, :], 2, ("ka", 0)), copy_to(ka[:, 1, :], 3, ("ka", 1))],
                     side_by_side(0, T, xn_hi, xn_lo, xn_ready)),
                pair(2, [values_part(j) for j in range(4)], [None, None, None, v_out]),
                pair(4, [xtile(j % 2) for j in range(4)], [copy_to(qb[:, j, :], j % 2, ("qb", j)) for j in range(4)]),
                pair(6, [xtile(0), token_tiles([1, 1, 1], [0, P, 2 * P]), xtile(0), xtile(1)],
                     [copy_to(kb[:, :], 0, "kb"), vb_out, r_out(0, 0), r_out(1, 1)]),
                pair(8, [xtile(j % 2) for j in range(4)],
                     [r_out(2, 0), r_out(3, 1), gate_out_dve(0, 0), gate_out_dve(1, 1)]),
            ]
            for i in range(3):
                pairs.append(pair(10 + 2 * i, [xtile(j % 2) for j in range(4)],
                                  [gate_out(2 + 4 * i + j, j % 2) for j in range(4)]))

            def of_a(bs):
                return half_tiles(bs, a_hi, a_lo, a_ready)

            def of_b(bs):
                return half_tiles(bs, b_hi, b_lo, b_ready)
            pairs.append(pair(16, [xtile(0), xtile(1), of_a(ab), of_a(cd)],
                              [gate_out(14, 0), last_gate, first_merged, merged_a([2, 3], cd)]))
            pairs.append(pair(18, [of_a(ab), of_a(cd), of_b(ab), of_b(cd)],
                              [merged_a([4, 5], ab), merged_a([6, 7], cd), merged_b([0, 1], ab), merged_b([2, 3], cd)]))
            pairs.append(pair(20, [of_b(ab), of_b(cd), ytile(0), ytile(1)],
                              [merged_b([4, 5], ab), merged_b([6, 7], cd), mixed_out(0, 0), mixed_out(1, 1)],
                              side_by_side(2, T, y_hi, y_lo, y_ready)))
            pairs.append(pair(22, [ytile(2), ytile(3), ytile(0), ytile(1)], [mixed_out(2 + j, (2 + j) % 4) for j in range(4)]))
            pairs.append(pair(24, [ytile(2), ytile(3)], [mixed_out(6, 2), mixed_out(7, 3)]))

            load_low_rank()
            ffn(0, v1[:, V_GAIN:V_GAIN + 8], pairs[0], small)
            before = all_so_far()
            normalise(TA, v1[:, V_GAIN + 8:V_GAIN + 16], held=pairs[0])
            clear_sumsq()
            need("act", before)
            need("dve", before)
            sides = [(1, 4, log_gates()), (6, 34, gla()), (8, 38, attention())]
            for i, p in enumerate(pairs):
                run_pair(p, pairs[i + 1] if i + 1 < len(pairs) else gate_up(1, 0), sides, at=4 * i, lead=p.lead is not None,
                         hold=i + 1 == len(pairs))
            xn_free[0] = S.unit_free[1]
            ffn(1, v1[:, V_GAIN + 16:V_GAIN + 24], first_pair((l + 1) * W1_ALL))

        ct.new_layer()
        with nc.Fori(0, L) as l:
            layer1(l)
            need("act", S.landed[1])
            ct.new_layer()
        TN = slice(0, N)

        fresh_layer()
        normalise(TB, vg[:, G_FN:G_FN + 8], into=lambda k, v: add_square_on_pe(k, TB, 6, v))
        keep_sumsq(TB, 6)

        place[0] = block_start
        v2 = sb("v2", [P, V2_ALL])
        mod = sb("mod", [P, 48])
        gain = sb("gain", [P, 2, KD])
        shared_start = place[0]
        f_hi = sb("f_hi", [P, KF2, N], F32R)
        f_lo = sb("f_lo", [P, KF2, N], F32R)
        place[0] = shared_start
        gates2 = sb("gates2", [P, 16, N])
        u_pool = sb("u_pool", [P, 4, T])
        s_pool = sb("s_pool", [P, 2, T])
        p_full = sb("p_full", [P, 4, N])
        p_hi = sb("p_hi", [P, 4, N], F32R)
        p_lo = sb("p_lo", [P, 4, N], F32R)
        cq = sb("cq", [P, 3, N])
        ckv = sb("ckv", [P, 2, N])
        cq_hi = sb("cq_hi", [P, 3, N], F32R)
        cq_lo = sb("cq_lo", [P, 3, N], F32R)
        ckv_hi = sb("ckv_hi", [P, 2, N], F32R)
        ckv_lo = sb("ckv_lo", [P, 2, N], F32R)
        k_rot = sb("k_rot", [96, N])
        q_all = sb("q_all", [96, MH, N])
        k_all = sb("k_all", [96, MH, N])
        v_tok = sb("v_tok", [P, 2, 512])
        r_tmp = sb("r_tmp", [96, 2, N])
        scores = sb("scores", [P, 2, 3 * P])
        pt2 = sb("pt2", [P, 2, 3 * P])
        stat2 = sb("stat2", [P, 32])
        a2_hi = sb("a2_hi", [P, 4, N], F32R)
        a2_lo = sb("a2_lo", [P, 4, N], F32R)
        pw_hi, pw_lo = p_hi, p_lo
        ct.new_layer()

        def layer2(l):
            fresh_layer()
            small = done("vec", sp.dma_start(v2[:, :], vec2[l]), 16)

            def w2_src(off, w, step=0, i=0):
                return weights[:, bass.ds(off + i * step + W2_AT + l * W2_ALL, w)]

            def block_pair(c, works, posts, widths, lead=None):
                n = len(works)
                return Pair([w2_src(M2_OFF[c], M2_WIDTH[c]), w2_src(M2_OFF[c + 1], M2_WIDTH[c + 1]) if widths[2] else None],
                            widths, works + [None] * (4 - n), posts + [None] * (4 - n), lead)

            ev = {}
            cq_ready, ckv_ready, p_ready, pw_ready, a2_ready, y_ready = [None] * 3, [None] * 2, [None] * 4, [None] * 4, [None] * 4, [None] * KD

            def xtile(b, rows=P, step=P):
                return feature_tile(b, rows, N, KD, xn_hi, xn_lo, xn_ready, step=step)

            def keep(dst, b, key, rows=slice(0, P), then=None):
                def post(m):
                    need("act", m)
                    ev[key] = A(act.activation(dst, bank[b][rows, 0:N], ACT.Copy))
                    evacuated(b, ev[key])
                    if then is not None:
                        then()
                return post

            def low_rank_norm(src, n_k, width, g0, hi, lo, ready, keys, b=7):
                need("dve", [ev[k] for k in keys], sq_free[1])
                for k in range(n_k):
                    dst = sq2 if k == 0 else gate[:, 0, :]
                    need("dve", gate_free2[0] if k else None)
                    v = V(dve.tensor_tensor(dst[:, 0:N], src[:, k, :], src[:, k, :], ALU.mult))
                    if k:
                        need("dve", v)
                        v = V(dve.tensor_tensor(sq2[:, 0:N], sq2[:, 0:N], gate[:, 0, 0:N], ALU.add))
                        need("dve", v)
                yield
                need("pe", v, bank_free[b])
                m = M(pe.matmul(bank[b][:, 0:N], ones, sq2[:, 0:N], start=True, stop=True))
                sq_free[1] = m
                r = inverse_root(gate[:, 1, 0:N], bank[b][:, 0:N], 1.0 / width, m, gate_free2[0])
                evacuated(b, r)
                need("dve", r)
                for k in range(n_k):
                    v = V(dve.scalar_tensor_tensor(out=src[:, k, :], in0=src[:, k, :], scalar=v2[:, g0 + k:g0 + k + 1],
                                                   in1=gate[:, 1, 0:N], op0=ALU.mult, op1=ALU.mult))
                    gate_free2[0] = v
                    ready[k] = split_rows(hi[:, k, :], lo[:, k, :], src[:, k, :], v)

            gate_free2 = [None]

            def k_rope():
                need("pe", ev["krope"], bank_free[6], bank_free[7])
                pe.matmul(bank[6][RP, 0:N], cst[0:32, C_ID:C_ID + 32], k_rot[0:32, :], start=True, stop=True)
                m = M(pe.matmul(bank[7][RP, 0:N], cst[0:32, C_R32:C_R32 + 32], k_rot[0:32, :], start=True, stop=True))
                need("dve", m, r_free[0])
                v = V(dve.tensor_tensor(r_tmp[RP, 0, :], bank[7][RP, 0:N], sin2[RP, :], ALU.mult))
                evacuated(7, v)
                w = V(dve.tensor_tensor(k_rot[RP, :], bank[6][RP, 0:N], cos2[RP, :], ALU.mult))
                evacuated(6, w)
                need("dve", w)
                v = V(dve.tensor_tensor(k_rot[RP, :], k_rot[RP, :], r_tmp[RP, 0, :], ALU.add))
                r_free[0] = v
                need("act", v)
                for h in range(MH):
                    e = A(act.activation(k_all[RP, h, :], k_rot[RP, :], ACT.Copy))
                ev["kr"] = e
                yield

            r_free = [None]

            def pooling():
                for g, w in enumerate(POOL_W):
                    need("pool", ev["pool", g])
                    cur = u_pool[:, g, :]
                    s, i = 1, 0
                    while s < w:
                        dst = s_pool[:, i, :]
                        p = G(pool.tensor_tensor(dst[:, META:T], cur[:, META:T], cur[:, META - s:T - s], ALU.add))
                        need("pool", p)
                        cur, s, i = dst, 2 * s, 1 - i
                    need("pool", ev.get("p_used"))
                    G(pool.tensor_tensor(p_full[:, g, 0:16], cur[:, META:META + 16], cst[:, C_CNT + 16 * g:C_CNT + 16 * g + 16], ALU.mult))
                    p = G(pool.tensor_scalar(p_full[:, g, 16:N], cur[:, META + 16:T], 1.0 / w, None, ALU.mult))
                    need("pool", p)
                    p = G(pool.tensor_tensor(p_full[:, g, :], p_full[:, g, :], u_pool[:, g, META:T], ALU.subtract))
                    need("pool", p)
                    ev["p", g] = p

            def pooled_split():
                for g in range(4):
                    p_ready[g] = split_rows(p_hi[:, g, :], p_lo[:, g, :], p_full[:, g, :], ev["p", g])

            def queries(h0, bs):
                def work(wh, wl):
                    for j in range(4):
                        b = bs[j]
                        need("pe", bank_free[b])
                        for k in range(3):
                            need("pe", cq_ready[k])
                            s = slice((3 * j + k) * QK, (3 * j + k + 1) * QK)
                            m = product(bank[b][0:QK, 0:N], wh[:, s], wl[:, s], cq_hi[:, k, :], cq_lo[:, k, :], k == 0, k == 2)
                    return m
                return work

            def queries_out(h0, bs):
                def post(m):
                    need("act", m)
                    for j in range(4):
                        e = A(act.activation(q_all[:, h0 + j, :], bank[bs[j]][0:QK, 0:N], ACT.Copy))
                        evacuated(bs[j], e)
                    ev["q", h0] = e
                return post

            def q_rope():
                for h in range(0, MH, 2):
                    h0 = h - h % 4
                    need("pe", ev["q", h0], bank_free[7])
                    m = M(pe.matmul(bank[7][RP, 0:2 * N], cst[RP, C_R32:C_R32 + 32],
                                    q_all[RP, h:h + 2, :].rearrange("p h n -> p (h n)"), start=True, stop=True))
                    need("dve", m, r_free[0])
                    for i in range(2):
                        v = V(dve.tensor_tensor(r_tmp[RP, i, :], bank[7][RP, i * N:(i + 1) * N], sin2[RP, :], ALU.mult))
                        w = V(dve.tensor_tensor(q_all[RP, h + i, :], q_all[RP, h + i, :], cos2[RP, :], ALU.mult))
                    evacuated(7, v)
                    need("dve", w)
                    v = V(dve.tensor_tensor(q_all[RP, h:h + 2, :], q_all[RP, h:h + 2, :], r_tmp[RP, :, :], ALU.add))
                    r_free[0] = v
                    ev["qr", h0] = v
                    yield

            def keys(wh, wl):
                for h in range(MH):
                    b = h // 2
                    need("pe", bank_free[b])
                    for k in range(2):
                        need("pe", ckv_ready[k])
                        s = slice((2 * h + k) * 64, (2 * h + k + 1) * 64)
                        m = product(bank[b][0:64, N * (h % 2):N * (h % 2) + N], wh[:, s], wl[:, s], ckv_hi[:, k, :], ckv_lo[:, k, :],
                                    k == 0, k == 1)
                return m

            def keys_out(m):
                need("act", m)
                for b in range(4):
                    e = A(act.activation(k_all[0:64, 2 * b:2 * b + 2, :].rearrange("p h n -> p (h n)"), bank[b][0:64, :], ACT.Copy))
                    evacuated(b, e)
                ev["k"] = e

            def values(wh, wl):
                for t in range(2):
                    need("pe", bank_free[t])
                    cs = slice(t * P, (t + 1) * P)
                    for k in range(2):
                        s = slice(k * 512, (k + 1) * 512)
                        pe.matmul(bank[t][:, :], ckv_hi[:, k, cs], wh[:, s], start=k == 0, stop=False)
                        pe.matmul(bank[t][:, :], ckv_lo[:, k, cs], wh[:, s], start=False, stop=False)
                        m = pe.matmul(bank[t][:, :], ckv_hi[:, k, cs], wl[:, s], start=False, stop=k == 1)
                return m

            def values_out(m):
                need("act", m)
                for t in range(2):
                    e = A(act.activation(v_tok[:, t, :], bank[t][:, :], ACT.Copy))
                    evacuated(t, e)
                ev["v"] = e

            def attention2():
                scale = QK ** -0.5
                p_free, t_free = [None, None], [None, None]
                bT, bO = 6, 7
                halves = (slice(0, P), slice(P, 3 * P))

                def softmax2(h):
                    j, bS = h % 2, 4 + h % 2
                    need("pe", ev["kr"], ev["k"], ev["qr", 4 * (h // 4)], bank_free[bS])
                    pe.matmul(bank[bS][:, 0:P], q_all[:, h, 0:P], k_all[:, h, 0:P], start=True, stop=True)
                    m = M(pe.matmul(bank[bS][:, P:3 * P], q_all[:, h, P:2 * P], k_all[:, h, :], start=True, stop=True))
                    need("dve", m, p_free[j])
                    c = 8 * (h % 4)
                    v = V(dve.tensor_tensor(scores[:, j, :], bank[bS][:, 0:3 * P], cst[:, C_MASK:C_MASK + 3 * P], ALU.add))
                    evacuated(bS, v)
                    need("dve", v)
                    for t, cs in enumerate(halves):
                        v = V(dve.reduce_max(stat2[:, c + t:c + t + 1], scores[:, j, cs], AX))
                    need("dve", v)
                    v = V(dve.tensor_scalar(stat2[:, c + 2:c + 4], stat2[:, c:c + 2], -scale, None, ALU.mult))
                    need("act", v)
                    for t, cs in enumerate(halves):
                        a = A(act.activation(scores[:, j, cs], scores[:, j, cs], ACT.Exp, bias=stat2[:, c + 2 + t:c + 3 + t],
                                             scale=scale, accum_out=stat2[:, c + 4 + t:c + 5 + t]))
                    need("dve", a)
                    v = V(dve.reciprocal(stat2[:, c + 6:c + 8], stat2[:, c + 4:c + 6]))
                    need("dve", v)
                    for t, cs in enumerate(halves):
                        v = V(dve.tensor_scalar(scores[:, j, cs], scores[:, j, cs], stat2[:, c + 6 + t:c + 7 + t], None, ALU.mult))
                    return v

                soft = None
                for h in range(MH + 1):
                    if h > 0:
                        j = (h - 1) % 2
                        need("pe", soft, bank_free[bT])
                        for t in range(3):
                            m = pe.transpose(bank[bT][:, t * P:(t + 1) * P], scores[:, j, t * P:(t + 1) * P], ident)
                        m = M(m)
                        p_free[j] = m
                        need("act", m, t_free[j])
                        a = A(act.activation(pt2[:, j, :], bank[bT][:, 0:3 * P], ACT.Copy))
                        evacuated(bT, a)
                    if h < MH:
                        soft = softmax2(h)
                    yield
                    if h > 0:
                        g = h - 1
                        need("pe", a, ev["v"], bank_free[bO] if j == 0 else None)
                        o = bank[bO][64 * j:64 * j + 64, :]
                        pe.matmul(o[:, 0:N], v_tok[:, 0, 64 * g:64 * g + 64], pt2[:, j, 0:2 * P], start=True, stop=False)
                        m = M(pe.matmul(o[:, P:N], v_tok[:, 1, 64 * g:64 * g + 64], pt2[:, j, 2 * P:3 * P], start=False, stop=True))
                        t_free[j] = m
                        if j:
                            a2_ready[g // 2] = split_rows(a2_hi[:, g // 2, :], a2_lo[:, g // 2, :], bank[bO][:, 0:N], m)
                            evacuated(bO, *a2_ready[g // 2])
                    if h < MH:
                        yield

            def gate2_out(j, b, then=None):
                return keep(gates2[:, j, :], b, ("g", j), then=then)

            def pool_out(g, b):
                def post(m):
                    need("act", m)
                    ev["pool", g] = A(act.activation(u_pool[:, g, META:T], bank[b][:, 0:N], ACT.Copy))
                    evacuated(b, ev["pool", g])
                return post

            def pool_project(wh, wl):
                for g in range(4):
                    b = g % 2
                    o = bank[b][:, N * (g // 2):N * (g // 2) + N]
                    need("pe", bank_free[b], p_ready[g])
                    s = slice(g * P, (g + 1) * P)
                    m = product(o, wh[:, s], wl[:, s], p_hi[:, g, :], p_lo[:, g, :], True, True)
                return m

            def pool_projected(m):
                need("act", m)
                for g in range(4):
                    o = bank[g % 2][:, N * (g // 2):N * (g // 2) + N]
                    a = A(act.activation(p_full[:, g, :], o, ACT.Copy, scale=v2[:, V_PS + g:V_PS + g + 1]))
                    evacuated(g % 2, a)
                    pw_ready[g] = split_rows(pw_hi[:, g, :], pw_lo[:, g, :], p_full[:, g, :], a)

            def half_tiles(bs, xh, xl, ready):
                def work(wh, wl):
                    for j, b in enumerate(bs):
                        need("pe", bank_free[b])
                        for k in range(4):
                            need("pe", ready[k])
                            s = slice((4 * j + k) * P, (4 * j + k + 1) * P)
                            m = product(bank[b][:, 0:N], wh[:, s], wl[:, s], xh[:, k, :], xl[:, k, :], k == 0, k == 3)
                    return m
                return work

            def merged_a(ms, bs):
                def post(m):
                    for mt, b in zip(ms, bs):
                        need("dve", m, ev["sig", 0])
                        v = V(dve.tensor_tensor(gates2[:, mt, :], gates2[:, mt, :], bank[b][:, 0:N], ALU.mult))
                        evacuated(b, v)
                        ev["ya", mt] = v
                return post

            def merged_b(ms, bs):
                def post(m):
                    for mt, b in zip(ms, bs):
                        need("dve", m, ev["ya", mt], ev["sig", 1])
                        v = V(dve.tensor_tensor(gates2[:, 8 + mt, :], gates2[:, 8 + mt, :], bank[b][:, 0:N], ALU.mult))
                        evacuated(b, v)
                    need("dve", v)
                    vs = [V(dve.tensor_tensor(gates2[:, mt, :], gates2[:, mt, :], gates2[:, 8 + mt, :], ALU.add)) for mt in ms]

                    def rest():
                        for mt, v in zip(ms, vs):
                            y_ready[mt] = split_rows(xn_hi[:, mt, TN], xn_lo[:, mt, TN], gates2[:, mt, :], v, xn_free[0])
                    return rest
                return post

            def residual(mt, b, g):
                def post(m):
                    need("dve", m)
                    v = V(dve.scalar_tensor_tensor(out=x[:, mt, TB], in0=bank[b][:, 0:N], scalar=mod[:, g + mt:g + mt + 1],
                                                   in1=x[:, mt, TB], op0=ALU.mult, op1=ALU.add))
                    evacuated(b, v)
                    add_squares(x[:, mt, TB], v, TB)
                return post

            def gates_sigmoid(half):
                g = gates2[:, 8 * half:8 * half + 8, :]
                need("act", ev["g", 15])
                ev["sig", half] = A(act.activation(g, g, ACT.Sigmoid))
                if half:
                    load_log_table()

            def gates_done():
                xn_free[0] = S.unit_free[3]
                gates_sigmoid(0)

            def first_merged(m):
                merged_a([0, 1], [0, 1])(m)
                gates_sigmoid(1)

            ab, cd = [0, 1], [2, 3]
            K4 = [1024] * 4

            def of_p(bs):
                return half_tiles(bs, pw_hi, pw_lo, pw_ready)

            def of_a(bs):
                return half_tiles(bs, a2_hi, a2_lo, a2_ready)

            def ytile(b):
                return feature_tile(b, P, N, KD, xn_hi, xn_lo, y_ready)

            pairs = [
                block_pair(0, [xtile(j) for j in range(4)],
                           [keep(cq[:, 0, :], 0, "cq0"), keep(cq[:, 1, :], 1, "cq1"),
                            keep(cq[:, 2, :], 2, "cq2"),
                            keep(ckv[:, 0, :], 3, "kv0")], K4, side_by_side(0, N, xn_hi, xn_lo, xn_ready)),
                block_pair(2, [xtile(0), xtile(1, 32, step=32), xtile(2), xtile(3)],
                           [keep(ckv[:, 1, :], 0, "kv1"),
                            keep(k_rot[0:32, :], 1, "krope", rows=slice(0, 32)),
                            pool_out(0, 2), pool_out(1, 3)], [1024, 256, 1024, 1024]),
                block_pair(4, [xtile(0), xtile(1), queries(0, [2, 3, 4, 5]), queries(4, [0, 1, 6, 2])],
                           [pool_out(2, 0), pool_out(3, 1), queries_out(0, [2, 3, 4, 5]), queries_out(4, [0, 1, 6, 2])],
                           [1024, 1024, 1152, 1152]),
                block_pair(6, [keys, values, xtile(2), xtile(3)],
                           [keys_out, values_out, gate2_out(0, 2), gate2_out(1, 3)], K4),
            ]
            for i in range(3):
                pairs.append(block_pair(8 + 2 * i, [xtile(j) for j in range(4)], [gate2_out(2 + 4 * i + j, j) for j in range(4)], K4))
            pairs.append(block_pair(14, [pool_project, None, xtile(2), xtile(3)],
                                    [pool_projected, None, gate2_out(14, 2), gate2_out(15, 3, then=gates_done)], [512, 0, 1024, 1024]))
            pairs.append(block_pair(16, [of_p(ab), of_p(cd), of_a(ab), of_a(cd)],
                                    [first_merged, merged_a([2, 3], cd),
                                     merged_b([0, 1], ab), merged_b([2, 3], cd)], K4))
            pairs.append(block_pair(18, [of_p(ab), of_p(cd), of_a(ab), of_a(cd)],
                                    [merged_a([4, 5], ab), merged_a([6, 7], cd), merged_b([4, 5], ab), merged_b([6, 7], cd)], K4))
            for i in range(2):
                pairs.append(block_pair(20 + 2 * i, [ytile(j) for j in range(4)], [residual(4 * i + j, j, 16) for j in range(4)], K4,
                                        side_by_side(0, N, xn_hi, xn_lo, y_ready) if i == 0 else None))

            f_ready = [None, None]

            def ff1(i):
                def squared(j):
                    def post(m):
                        q = j % 2
                        need("dve", m, full_free[q])
                        v = V(dve.tensor_scalar(full[:, q, 0:N], bank[j][:, 0:N], 0.0, None, ALU.max))
                        evacuated(j, v)
                        need("dve", v)
                        v = V(dve.tensor_tensor(full[:, q, 0:N], full[:, q, 0:N], full[:, q, 0:N], ALU.mult))
                        hh, hl = f_hi[:, bass.ds(4 * i + j, 1), :], f_lo[:, bass.ds(4 * i + j, 1), :]
                        fj = full[:, q:q + 1, 0:N]

                        def rest():
                            full_free[q] = split_rows(hh, hl, fj, v)
                            if j == 0:
                                f_ready[0] = f_ready[1]
                            f_ready[1] = full_free[q]
                        return rest
                    return post
                return Pair([w2_src(W2_FF1, 2048, 4096, i), w2_src(W2_FF1 + 2048, 2048, 4096, i)], K4,
                            [xtile(j) for j in range(4)], [squared(j) for j in range(4)], side_by_side(0, N, xn_hi, xn_lo, xn_ready))

            def ff2(g, half):
                def part(c, j):
                    def work(wh, wl):
                        b = 4 + j
                        if half == 0 and c == 0:
                            need("pe", bank_free[b])
                        need("pe", f_ready[half])
                        for k in range(8):
                            kk = 16 * half + 8 * c + k
                            s = slice(k * P, (k + 1) * P)
                            m = product(bank[b][:, 0:N], wh[:, s], wl[:, s], f_hi[:, kk, :], f_lo[:, kk, :], kk == 0, kk == KF2 - 1)
                        return m
                    return work

                def add(j):
                    def post(m):
                        xk = x[:, bass.ds(2 * g + j, 1), TB]
                        need("dve", m)
                        o = bank[4 + j][:, 0:N].rearrange("p (a t) -> p a t", a=1)
                        v = V(dve.tensor_scalar(full[:, 0:1, 0:N], o, mod[:, bass.ds(40 + 2 * g + j, 1)], None, ALU.mult))
                        evacuated(4 + j, v)
                        need("dve", v)
                        v = V(dve.tensor_tensor(xk, xk, full[:, 0:1, 0:N], ALU.add))
                        add_squares(xk.rearrange("p a t -> p (a t)"), v, TB)
                    return post
                o = W2_FF2 + half * 4096
                return Pair([w2_src(o, 2048, 8192, g), w2_src(o + 2048, 2048, 8192, g)], K4,
                            [part(0, 0), part(0, 1), part(1, 0), part(1, 1)], [None, None] + ([add(0), add(1)] if half else [None, None]))

            for b in (u_pool, s_pool):
                z = G(pool.memset(b[:, :, 0:META], 0.0))
            need("pool", z)
            v = V(dve.tensor_copy(mod[:, :].rearrange("p (a n) -> p a n", a=1), mod_all[:, bass.ds(l, 1), :]))
            need("dve", v, small)
            for i, (g, sc) in enumerate(((V_LN1, 8), (V_LN2, 32))):
                v = V(dve.scalar_tensor_tensor(out=gain[:, i, :], in0=mod[:, sc:sc + 8], scalar=1.0, in1=v2[:, g:g + 8],
                                               op0=ALU.add, op1=ALU.mult))
            normalise(TB, gain[:, 0, :], mod[:, 0:8], held=pairs[0], gain_ready=[v, small])
            clear_sumsq()
            sides = [(4, 10, low_rank_norm(cq, 3, QL, V_QG, cq_hi, cq_lo, cq_ready, ["cq0", "cq1", "cq2"])),
                     (6, 12, low_rank_norm(ckv, 2, KVL, V_KVG, ckv_hi, ckv_lo, ckv_ready, ["kv0", "kv1"])),
                     (8, 12, k_rope()), (10, 14, q_rope()), (13, 31, attention2())]
            for i, p in enumerate(pairs):
                if i == 3:
                    pooling()
                if i == 5:
                    pooled_split()
                run_pair(p, pairs[i + 1] if i + 1 < len(pairs) else ff1(0), sides, at=4 * i, lead=p.lead is not None,
                         hold=i + 1 == len(pairs))
            xn_free[0] = S.unit_free[3]
            before = all_so_far()
            normalise(TB, gain[:, 1, :], mod[:, 24:32], held=ff1(0))
            clear_sumsq()
            need("act", before)
            need("dve", before)
            ct.repeat(8, lambda i: run_pair(ff1(i), ff2(0, 0) if isinstance(i, int) and i == 7 else ff1(i + 1),
                                           lead=isinstance(i, int) and i == 0))

            def last_step(g):
                run_pair(ff2(g, 0), ff2(g, 1))
                last = isinstance(g, int) and g == 3
                if last:
                    load_log_table()
                run_pair(ff2(g, 1), first_pair(W2_AT + (l + 1) * W2_ALL) if last else ff2(g + 1, 0), hold=last)
            ct.repeat(4, last_step)

        with nc.Fori(0, L) as l2:
            layer2(l2)
            need("act", S.landed[1])
            ct.new_layer()

        fresh_layer()
        normalise(TB, vg[:, G_FG:G_FG + 8], into=lambda k, v: (
            need("sp", v), sp.dma_start(out[:, k, :], x[:, k, TB]).then_inc(ct.out_sem, 16)))
        sp.wait_ge(ct.out_sem, 16 * KD)


def _units(w, cols):
    k = w.shape[0] // P
    w = w.reshape(k, P, w.shape[1] // cols, cols)
    return w.transpose(1, 2, 0, 3).reshape(P, -1)


def _columns(v):
    return v.reshape(-1, P).T


def _layer1_weights(i, l):
    parts = []
    for f in range(2):
        g, u = _units(i["ffn_w_gate"][l, f], P), _units(i["ffn_w_up"][l, f], P)
        gu = np.stack([g.reshape(P, FG, 2048), u.reshape(P, FG, 2048)], axis=2).reshape(P, -1)
        dn = i["ffn_w_down"][l, f].reshape(2, KF // 2, P, 4, 2, P)
        dn = dn.transpose(2, 3, 0, 4, 1, 5).reshape(P, -1)
        if f == 0:
            w = i["w_in"][l]
            a = w[:, 0:1536]
            b = w[:, 1568:]
            pa, pb = _units(i["w_pa"][l], P), _units(i["w_pb"][l], P)
            mix = [_units(a[:, 0:512], P), _units(a[:, 512:1024], 512), _units(b[:, 0:512], P), _units(b[:, 512:768], P), _units(a[:, 1024:1536], P),
                   _units(b[:, 768:], P), pa[:, 0:2048], pa[:, 2048:], pb[:, 0:2048], pb[:, 2048:], _units(i["w_out"][l], P)]
            parts += [gu, dn] + mix
        else:
            parts += [gu, dn]
    return np.concatenate(parts, axis=1)


def _constants():
    c = np.zeros((P, C_ALL), np.float32)
    c[:, C_ID:C_ID + P] = np.eye(P)
    c[:, C_ONE:C_ONE + P] = 1
    j, i = np.arange(P)[:, None], np.arange(P)[None, :]
    same = j // CHUNK == i // CHUNK
    c[:, C_BLK:C_BLK + P] = same
    c[:, C_CUM[0]:C_CUM[0] + P] = (same & (j <= i)) / 16.0
    c[:, C_CUM[1]:C_CUM[1] + P] = (same & (j >= i)) / 16.0
    c[:, C_END[0]:C_END[0] + P] = (same & (j > i)) / 16.0
    c[:, C_END[1]:C_END[1] + P] = (same & (j < i)) / 16.0
    rot = np.zeros((P, P), np.float32)
    for s in range(0, P, 32):
        for q in range(16):
            rot[s + q, s + q + 16] = -1
            rot[s + q + 16, s + q] = 1
    c[:, C_ROT:C_ROT + P] = rot.T
    for g in range(2):
        dup = np.zeros((P, P), np.float32)
        for q in range(P):
            dup[q, 64 * g + q % 64] = 1
        c[:, C_DUP[g]:C_DUP[g] + P] = dup.T
        c[:, C_DROT[g]:C_DROT[g] + P] = (dup @ rot).T
    f32 = np.float32
    row, col = np.repeat(np.arange(SEQ // 64), 64).astype(f32), np.tile(np.arange(64), SEQ // 64).astype(f32)
    inv = (f32(10000.0) ** (-np.arange(0, 32, 2, dtype=f32) / f32(32))).astype(f32)
    ang = np.concatenate([row[:, None] * inv, col[:, None] * inv], axis=-1)
    ang = np.concatenate([np.zeros((META, 32), f32), ang], axis=0)
    d = np.arange(P) % 64
    which = (d // 32) * 16 + d % 16
    c[:, C_COS:C_COS + T] = np.cos(ang).T[which]
    c[:, C_SIN:C_SIN + T] = np.sin(ang).T[which]
    r32 = np.zeros((32, 32), np.float32)
    for q in range(16):
        r32[q, q + 16] = -1
        r32[q + 16, q] = 1
    c[0:32, C_R32:C_R32 + 32] = c[64:96, C_R32:C_R32 + 32] = r32.T
    inv2 = (f32(10000.0) ** (-np.arange(0, 32, 2, dtype=f32) / f32(32))).astype(f32)
    c[64:96, C_INV] = np.concatenate([inv2, inv2])
    m = np.where(j >= i, 0.0, np.finfo(np.float32).min)
    c[:, C_MASK:C_MASK + P] = m
    c[:, C_MASK + 2 * P:C_MASK + 3 * P] = m
    t = np.arange(16)
    for g, w in enumerate(POOL_W):
        c[:, C_CNT + 16 * g:C_CNT + 16 * g + 16] = 1.0 / np.minimum(t + 1, w)
    c[:, C_EPS] = EPS
    k = np.zeros((P, 2, T), np.int32)
    for c0, n in TILES:
        jj, ii = np.arange(n)[:, None], np.arange(n)[None, :]
        s = jj // CHUNK == ii // CHUNK
        k[0:n, 0, c0:c0 + n] = s & (jj <= ii)
        k[0:n, 1, c0:c0 + n] = s & (jj >= ii)
    return c, k.reshape(P, 2 * T)


def _layout(inp):
    i = {k: np.asarray(v) for k, v in inp.items()}
    f = {}
    h = np.concatenate([i["meta_tokens"], i["x"][0]], axis=0)
    f["x0"] = h.T.reshape(KD, P, T).transpose(1, 0, 2).reshape(P, KD * T)
    w2 = np.zeros((L, 33, 512), np.float32)
    w2[:, 0:16, 0:256] = i["gla_w2"][:, 0]
    w2[:, 16:32, 256:512] = i["gla_w2"][:, 1]
    w2[:, 32, :] = i["gla_b2"].reshape(L, 512)
    f["w2cat"] = w2
    f["lr_w"] = np.stack([_units(i["w_in"][l][:, 1536:1568], 32) for l in range(L)])
    f["vec1"] = np.stack([np.concatenate([
        _columns(i["norm_gains"][l].reshape(-1)), _columns(i["b_merge"][l].reshape(-1)), _columns(i["gla_gn"][l]),
        np.concatenate([i["q_norm"][l]] * 2)[:, None], np.concatenate([i["k_norm"][l]] * 2)[:, None]], axis=1) for l in range(L)])
    f["vecg"] = np.concatenate([_columns(i["final_norm"]), _columns(i["final_g_2"]), _columns(i["c_2"][0])], axis=1)
    a = i["w_ada_2"].reshape(L, 2, 4, P, 12, 512).transpose(0, 3, 1, 4, 2, 5)
    f["ada_w"] = a.reshape(L, P, 24 * 2048)
    f["b_ada"] = np.stack([_columns(i["b_ada_2"][l]) for l in range(L)])
    w2, f["vec2"] = _layer2(i)
    f["weights"] = np.concatenate([_layer1_weights(i, l) for l in range(L)] + w2 + [np.zeros((P, 2 * FIRST_W), np.float32)], axis=1)
    f["pos"] = np.broadcast_to(i["positions_2"], (32, SEQ))
    f["const"], f["masks"] = _constants()
    return {k: np.ascontiguousarray(v) for k, v in f.items()}


def _layer2(i):
    ws, vs = [], []
    for l in range(L):
        w = i["w_in_2"][l]
        uq = i["w_uq_2"][l].reshape(QL, MH * QK)
        uk = i["w_uk_2"][l].reshape(KVL, 512)
        uv = i["w_uv_2"][l].reshape(KVL, 512)
        pp, pa = _units(i["p_pool_2"][l], P), _units(i["p_attn_2"][l], P)
        parts = [_units(w[:, 512:1152], P), _units(w[:, 1152:1184], 32), _units(w[:, 0:512], P), _units(uq, QK),
                 _units(uk, 64), _units(uv, 512), _units(w[:, 1184:1184 + 14 * P], P),
                 i["w_pool_2"][l].transpose(1, 0, 2).reshape(P, 512), _units(w[:, 1184 + 14 * P:], P),
                 pp[:, 0:2048], pa[:, 0:2048], pp[:, 2048:], pa[:, 2048:], _units(i["w_out_2"][l], P),
                 _units(i["w_ff1_2"][l], P)]
        f2 = i["w_ff2_2"][l].reshape(4, 8, P, 4, 2, P).transpose(2, 3, 0, 4, 1, 5).reshape(P, -1)
        ws.append(np.concatenate(parts + [f2], axis=1))
        vs.append(np.concatenate([_columns(i["ln1_g_2"][l]), _columns(i["ln2_g_2"][l]), _columns(i["q_norm_g_2"][l]),
                                  _columns(i["kv_norm_g_2"][l]), _columns(i["pool_scale_2"][l])], axis=1))
    return ws, np.stack(vs)


_NAMES = ["x0", "weights", "w2cat", "lr_w", "vec1", "vec2", "vecg", "ada_w", "b_ada", "pos", "const", "masks"]


def kernel(**inputs):
    import concourse.bacc as bacc
    from concourse.bass_utils import run_bass_kernel_spmd

    nc = bacc.Bacc("TRN2", target_bir_lowering=False, num_devices=1)
    laid = _layout(inputs)
    arrays, args = {}, {}
    for name in _NAMES:
        a = laid[name]
        arrays[f"in_{name}"] = a
        args[name] = nc.dram_tensor(f"in_{name}", a.shape, mybir.dt.from_np(a.dtype), kind="ExternalInput").ap()
    args["out"] = nc.dram_tensor("out_0", (P, KD, SEQ), F32, kind="ExternalOutput").ap()
    program(nc, **args)
    r = run_bass_kernel_spmd(nc, [arrays], core_ids=[0])
    y = r.results[0]["out_0"]
    return y.transpose(2, 1, 0).reshape(1, SEQ, D)
```
